# Optimizing a Trainium2 kernel written in Bass

```python
import jax, jax.numpy as jnp
from jax import lax
import numpy as np

D_MODEL = 1024
BATCH = 1
SEQ = 256
DEPTH = 1

CHUNK = 64
N_ATTN_HEADS = 8
HEAD_DIM = 64
D_ATTN = N_ATTN_HEADS * HEAD_DIM
LEFT_CHUNKS = 8
BAND = (LEFT_CHUNKS + 1) * CHUNK
REL_MAX = 128
REL_MIN = -(CHUNK - 1)
N_REL = REL_MAX - REL_MIN + 1
D_CONV = D_MODEL - D_ATTN
CONV_WIDTH = 31
D_MIX = D_ATTN + D_CONV
D_IN_COLS = 3 * D_ATTN + 2 * D_CONV
N_EXPERTS = 32
TOP_K = 4
D_EXPERT = D_MODEL
SWIGLU_ALPHA = 1.702
SWIGLU_LIMIT = 7.0
RMS_EPS = 1e-5
LN_EPS = 1e-5

kernel_name = "hymba_conformer_chunkattn_moe_block"

def rms_norm(x, g):
    xf = x.astype(jnp.float32)
    y = xf * lax.rsqrt(jnp.mean(xf * xf, axis=-1, keepdims=True) + RMS_EPS)
    return (y * g.astype(jnp.float32)).astype(x.dtype)

def layer_norm(x, g, b):
    xf = x.astype(jnp.float32)
    mu = jnp.mean(xf, axis=-1, keepdims=True)
    var = jnp.mean(jnp.square(xf - mu), axis=-1, keepdims=True)
    y = (xf - mu) * lax.rsqrt(var + LN_EPS)
    return (y * g.astype(jnp.float32) + b.astype(jnp.float32)).astype(x.dtype)

def chunked_rel_attention(q, k, v, rel_bias):
    b, s, h, dh = q.shape
    nc = s // CHUNK
    qc = q.reshape(b, nc, CHUNK, h, dh)
    pad = ((0, 0), (LEFT_CHUNKS * CHUNK, 0), (0, 0), (0, 0))
    kp = jnp.pad(k, pad).reshape(b, nc + LEFT_CHUNKS, CHUNK, h, dh)
    vp = jnp.pad(v, pad).reshape(b, nc + LEFT_CHUNKS, CHUNK, h, dh)
    k_band = jnp.concatenate([kp[:, j:j + nc] for j in range(LEFT_CHUNKS + 1)], axis=2)
    v_band = jnp.concatenate([vp[:, j:j + nc] for j in range(LEFT_CHUNKS + 1)], axis=2)

    iq = jnp.arange(CHUNK)[:, None]
    kk = jnp.arange(BAND)[None, :]
    dist = iq + LEFT_CHUNKS * CHUNK - kk
    idx = jnp.clip(dist, REL_MIN, REL_MAX) - REL_MIN
    bias = rel_bias[:, idx].astype(jnp.float32)

    chunk_of_key = jnp.arange(nc)[:, None] - LEFT_CHUNKS + jnp.arange(BAND)[None, :] // CHUNK
    valid = chunk_of_key >= 0

    scale = HEAD_DIM ** -0.5
    scores = jnp.einsum('bcqhd,bckhd->bchqk', qc, k_band).astype(jnp.float32) * scale
    scores = scores + bias[None, None]
    scores = jnp.where(valid[None, :, None, None, :], scores, -jnp.inf)
    probs = jax.nn.softmax(scores, axis=-1).astype(v.dtype)
    out = jnp.einsum('bchqk,bckhd->bcqhd', probs, v_band)
    return out.reshape(b, s, h * dh)

def conformer_conv(u, dw_w, dw_b, ln_g, ln_b):
    a, gate = jnp.split(u, 2, axis=-1)
    hcv = a * jax.nn.sigmoid(gate)
    hcv = lax.conv_general_dilated(
        hcv, dw_w[:, None, :].astype(hcv.dtype),
        window_strides=(1,),
        padding=((CONV_WIDTH - 1, 0),),
        dimension_numbers=('NWC', 'WIO', 'NWC'),
        feature_group_count=D_CONV) + dw_b
    hcv = layer_norm(hcv, ln_g, ln_b)
    return jax.nn.silu(hcv)

def clamped_swiglu_expert(t, wg, bg, wu, bu, wd, bd):
    gate = jnp.minimum(t @ wg + bg, SWIGLU_LIMIT)
    up = jnp.clip(t @ wu + bu, -SWIGLU_LIMIT, SWIGLU_LIMIT)
    hid = (up + 1.0) * (gate * jax.nn.sigmoid(SWIGLU_ALPHA * gate))
    return hid @ wd + bd

def moe_ffn(x, router_w, router_b, w_gate, b_gate, w_up, b_up, w_down, b_down):
    b, s, d = x.shape
    t = x.reshape(b * s, d)
    logits = (t @ router_w + router_b).astype(jnp.float32)
    top_val, top_idx = lax.top_k(logits, TOP_K)
    top_w = jax.nn.softmax(top_val, axis=-1)
    combine = jnp.sum(jax.nn.one_hot(top_idx, N_EXPERTS, dtype=jnp.float32) * top_w[..., None], axis=1)
    combine = combine.astype(x.dtype)
    y = jnp.zeros_like(t)
    for e in range(N_EXPERTS):
        y = y + combine[:, e:e + 1] * clamped_swiglu_expert(
            t, w_gate[e], b_gate[e], w_up[e], b_up[e], w_down[e], b_down[e])
    return y.reshape(b, s, d)

def setup_inputs(seed: int = 0) -> dict:
    key = jax.random.key(seed)
    ks = jax.random.split(key, 20)
    f32 = jnp.float32
    L = DEPTH

    def nrm(k, shape, scale):
        return scale * jax.random.normal(k, shape, f32)

    return {
        "x": nrm(ks[0], (BATCH, SEQ, D_MODEL), 1.0),
        "norm_mix_g": 1.0 + nrm(ks[1], (L, D_MODEL), 0.02),
        "w_in": nrm(ks[2], (L, D_MODEL, D_IN_COLS), D_MODEL ** -0.5),
        "conv_dw_w": nrm(ks[3], (L, CONV_WIDTH, D_CONV), CONV_WIDTH ** -0.5),
        "conv_dw_b": nrm(ks[4], (L, D_CONV), 0.02),
        "conv_ln_g": 1.0 + nrm(ks[5], (L, D_CONV), 0.02),
        "conv_ln_b": nrm(ks[6], (L, D_CONV), 0.02),
        "rel_bias": nrm(ks[7], (L, N_ATTN_HEADS, N_REL), 0.1),
        "w_out": nrm(ks[8], (L, D_MIX, D_MODEL), D_MIX ** -0.5),
        "norm_ffn_g": 1.0 + nrm(ks[9], (L, D_MODEL), 0.02),
        "router_w": nrm(ks[10], (L, D_MODEL, N_EXPERTS), D_MODEL ** -0.5),
        "router_b": nrm(ks[11], (L, N_EXPERTS), 0.01),
        "exp_w_gate": nrm(ks[12], (L, N_EXPERTS, D_MODEL, D_EXPERT), D_MODEL ** -0.5),
        "exp_b_gate": nrm(ks[13], (L, N_EXPERTS, D_EXPERT), 0.02),
        "exp_w_up": nrm(ks[14], (L, N_EXPERTS, D_MODEL, D_EXPERT), D_MODEL ** -0.5),
        "exp_b_up": nrm(ks[15], (L, N_EXPERTS, D_EXPERT), 0.02),
        "exp_w_down": nrm(ks[16], (L, N_EXPERTS, D_EXPERT, D_MODEL), D_EXPERT ** -0.5),
        "exp_b_down": nrm(ks[17], (L, N_EXPERTS, D_MODEL), 0.02),
        "norm_final_g": 1.0 + nrm(ks[18], (D_MODEL,), 0.02),
    }

def reference(x, norm_mix_g, w_in, conv_dw_w, conv_dw_b, conv_ln_g, conv_ln_b, rel_bias,
              w_out, norm_ffn_g, router_w, router_b, exp_w_gate, exp_b_gate, exp_w_up,
              exp_b_up, exp_w_down, exp_b_down, norm_final_g):
    b, s, _ = x.shape
    for l in range(DEPTH):
        h = rms_norm(x, norm_mix_g[l])
        proj = h @ w_in[l]
        q, k, v, conv_in = jnp.split(proj, [D_ATTN, 2 * D_ATTN, 3 * D_ATTN], axis=-1)
        q = q.reshape(b, s, N_ATTN_HEADS, HEAD_DIM)
        k = k.reshape(b, s, N_ATTN_HEADS, HEAD_DIM)
        v = v.reshape(b, s, N_ATTN_HEADS, HEAD_DIM)
        attn_out = chunked_rel_attention(q, k, v, rel_bias[l])
        conv_out = conformer_conv(conv_in, conv_dw_w[l], conv_dw_b[l],
                                  conv_ln_g[l], conv_ln_b[l])
        mixed = jnp.concatenate([attn_out, conv_out], axis=-1) @ w_out[l]
        x = x + mixed
        x = x + moe_ffn(rms_norm(x, norm_ffn_g[l]), router_w[l], router_b[l],
                        exp_w_gate[l], exp_b_gate[l], exp_w_up[l], exp_b_up[l],
                        exp_w_down[l], exp_b_down[l])
    return rms_norm(x, norm_final_g)


_drawn_inputs = setup_inputs


def setup_inputs(seed=0):
    import zlib

    import numpy as np

    out = dict(_drawn_inputs(seed))
    spreads = {}
    factors = {'exp_b_gate': 6.565, 'exp_b_up': 8.0, 'exp_b_down': 6.317, 'norm_final_g': 2.904}
    for name, (base, spread) in spreads.items():
        noise = np.random.default_rng([zlib.crc32(name.encode()), seed]).standard_normal(out[name].shape)
        drawn = base * np.exp(spread * noise) if base else spread * noise
        out[name] = __import__('jax').numpy.asarray(drawn.astype(out[name].dtype))
    for name, factor in factors.items():
        out[name] = (out[name] * factor).astype(out[name].dtype)
    return out
```

```python
from contextlib import ExitStack

import concourse.bass as bass
from concourse import mybir

P = 128
F32 = mybir.dt.float32
I32 = mybir.dt.int32
U32 = mybir.dt.uint32
ALU = mybir.AluOpType
ACT = mybir.ActivationFunctionType
AX = mybir.AxisListType

D = 1024
T = 256
KT = D // P
TT = T // P
HEADS, HD = 8, 64
D_ATTN = HEADS * HD
D_CONV = 512
CC = D_CONV // P
TAPS = 31
PAD = TAPS - 1
E = 32
TOPK = 4
CAP = 64
EXTRA = T // CAP - 1
PAIRS = E // 2
LIMIT = 7.0
ALPHA = 1.702
EPS = 1e-5
MASKED = -1e30
HB = 512


class Steps:

    def __init__(self, eng, sem):
        self.eng, self.sem, self.n = eng, sem, 0

    def mark(self, ins):
        ins.then_inc(self.sem, 1)
        self.n += 1
        return self.n

    def wait(self, n=None):
        self.eng.wait_ge(self.sem, self.n if n is None else n)


def build_block(nc, a, out):
    with ExitStack() as ctx:
        def sb(name, shape, dt=F32):
            return ctx.enter_context(nc.sbuf_tensor(name, shape, dt))

        def psum(name, shape):
            return ctx.enter_context(nc.psum_tensor(name, shape, F32))

        def sem(name):
            return ctx.enter_context(nc.semaphore(name))

        y = psum("y", [P, 2 * TT, HB])
        b4, b5, b6, b7 = (psum(f"b{i}", [P, HB]) for i in range(4, 8))
        bank = [b4, b5, b6, b7]

        slot = sb("slot", [P, 5, KT, D])
        GATE, UP, DOWN = (0, 3), (1, 4), (2, 2)
        work = sb("work", [P, 6392])
        h2 = sb("h2", [P, TT, D])
        late = sb("late", [P, D])
        probsT = sb("probsT", [P, 2, 3 * P])
        router_w = sb("router_w", [P, KT, E])
        router_b = sb("router_b", [P, E])
        ident_w = sb("ident_w", [P, P + 2])
        ident = ident_w[:, 0:P]
        ones = sb("ones", [P, P])
        before = sb("before", [P, P])
        iota = sb("iota", [P, T])
        bias_gu = sb("bias_gu", [P, HB])
        rank = sb("rank", [P, TT, E + 2])
        share = sb("share", [P, TT, E + 2])
        cols = sb("cols", [P, KT + CC * TAPS + 3 * CC])
        sm = sb("sm", [P, 64])
        meta = sb("meta", [1, 2 * EXTRA * E + 8], I32)

        def part(t, at, shape):
            n = 1
            for s in shape:
                n *= s
            v = t[:, at:at + n]
            if len(shape) == 1:
                return v
            names = "abc"[:len(shape)]
            return v.rearrange(f"p ({' '.join(names)}) -> p {' '.join(names)}",
                               **{c: s for c, s in zip(names[1:], shape[1:])})

        xg = part(work, 0, [KT, 2 * CAP])
        hid = part(work, 1024, [HB])
        hidT = part(work, 1536, [4, P])
        gate = part(work, 2048, [HB])
        up = part(work, 2560, [HB])
        yg = part(work, 3072, [2, HB])
        sel = part(work, 4216, [TT, 2 * CAP])
        wsel = part(work, 4472, [TT, 3 * CAP])
        wselT = part(work, 4856, [2, T])
        pick = part(work, 5368, [2, 4, CAP])
        sig = part(work, 5880, [HB])
        hT = part(work, 0, [KT, T])
        rstd_row = part(work, 2048, [T])
        val = part(work, 2048, [TT, D_ATTN])
        gain_ffn = part(work, 2048, [D])
        padded = part(work, 3072, [CC, PAD + T])
        lnsq = part(work, 3072, [CC, T])
        mixT = part(work, 4216, [2 * CC, T])
        xsq = part(work, 4216, [KT, T])
        h2f = h2[:].rearrange("p t d -> p (t d)")
        xT = part(h2f, 0, [KT, T])
        acc = part(h2f, 0, [CC, T])
        sgate = part(h2f, 1024, [CC, T])
        lnrow = part(h2f, 1024, [CC, T])
        probs = part(late, 0, [2, 3 * P])
        lgT = part(late, 0, [T])
        lg = part(late, 256, [TT, E])
        hit = part(late, 320, [TT * TOPK, E])
        whit = part(late, 576, [TT * TOPK, E])
        mask = part(late, 832, [TT, E])
        mask3 = part(late, 0, [TT, EXTRA * E])
        w_conv = slot[:, 4].rearrange("p a b -> p (a b)").rearrange("p (c k n) -> p c k n", c=CC, k=KT)
        w_qk = slot[:, 3].rearrange("p a b -> p (a b)").rearrange("p (c k n) -> p c k n", c=4, k=KT)
        w_out = slot[:, 4]
        s2 = slot[:, 2].rearrange("p a b -> p (a b)")
        w_v = s2[:, 0:4096].rearrange("p (k n) -> p k n", k=KT)
        x_tok = s2[:, 0:TT * D].rearrange("p (t d) -> p t d", t=TT)
        qkT = s2[:, 4096:6144].rearrange("p (c w t) -> p c w t", c=4, w=2)
        relb = s2[:, 6144:8192].rearrange("p (h k) -> p h k", h=HEADS)
        outb = slot[:, 0].rearrange("p a b -> p (a b)")[:, 0:TT * D].rearrange("p (t d) -> p t d", t=TT)
        g_mix = cols[:, 0:KT]
        dw = cols[:, KT:KT + CC * TAPS].rearrange("p (c k) -> p c k", c=CC)
        c0 = KT + CC * TAPS
        dw_b, ln_g, ln_b = (cols[:, c0 + i * CC:c0 + (i + 1) * CC] for i in range(3))
        negmax, den, rden = sm[:, 0:4], sm[:, 4:8], sm[:, 8:12]
        ssq, rstd = sm[:, 12:14], sm[:, 14:16]
        fsq, frstd = sm[:, 16:18], sm[:, 18:20]
        topv = sm[:, 20:36].rearrange("p (t k) -> p t k", t=TT)
        topw = sm[:, 36:44].rearrange("p (t k) -> p t k", t=TT)
        topi = sb("topi", [P, TT, 8], U32)
        topf = sm[:, 44:52].rearrange("p (t k) -> p t k", t=TT)
        wsum = sm[:, 52:54]
        code_e, code_c, thresh, flag, place = (sm[:, 54 + i:55 + i] for i in range(5))
        onehot = part(late, TT * EXTRA * E, [EXTRA * E])

        d_xT, d_cols, d_qk, d_v, d_wout, d_xtok, d_rel, d_small, d_gffn, d_bias, d_yg, d_gfin, d_out = (
            sem(f"d_{n}") for n in ("xT", "cols", "qk", "v", "wout", "xtok", "rel", "small", "gffn",
                                    "bias", "yg", "gfin", "out"))
        d_conv = [sem(f"d_conv{c}") for c in range(CC)]
        d_slot = [[sem(f"d_slot{s}{h}") for h in range(2)] for s in range(5)]
        const_ready, cleared = sem("const_ready"), sem("cleared")
        pool_step, dve_step, act_step = sem("pool_step"), sem("dve_step"), sem("act_step")
        dve_tail, dve_over = sem("dve_tail"), sem("dve_over")
        sq_ready, ssum_done, var_ready, sd_ready = (sem(n) for n in ("sq_ready", "ssum_done", "var_ready", "sd_ready"))
        hT_ready, conv_mm, sgate_ready, conv_read = (sem(n) for n in ("hT_ready", "conv_mm", "sgate_ready", "conv_read"))
        qk_mm, qk_ready, v_mm, v_ready = (sem(n) for n in ("qk_mm", "qk_ready", "v_mm", "v_ready"))
        acc_ready, mu_mm, cent_ready, lnsq_ready, lnv_mm, lnv_ready, lnsd_ready, xn_ready, lnsig_ready, conv_ready = (
            sem(n) for n in ("acc_ready", "mu_mm", "cent_ready", "lnsq_ready", "lnv_mm", "lnv_ready",
                             "lnsd_ready", "xn_ready", "lnsig_ready", "conv_ready"))
        score_mm, score_read, max_ready, exp_ready, probs_ready, probsT_mm, probsT_ready, av_mm, av_ready = (
            sem(n) for n in ("score_mm", "score_read", "max_ready", "exp_ready", "probs_ready", "probsT_mm",
                             "probsT_ready", "av_mm", "av_ready"))
        out_mm, ssq_ready, ms_ready, rms_sd, h2_ready, h2T_mm, h2T_act, h2T_dve, lg_mm, lgT_ready, lgt_mm = (
            sem(n) for n in ("out_mm", "ssq_ready", "ms_ready", "rms_sd", "h2_ready", "h2T_mm", "h2T_act",
                             "h2T_dve", "lg_mm", "lgT_ready", "lgt_mm"))
        top_shift, top_exp, mask_ready, rank_mm, cnt_mm, flag_ready, place_mm, onehot_ready, list_mm, meta_ready = (
            sem(n) for n in ("top_shift", "top_exp", "mask_ready", "rank_mm", "cnt_mm", "flag_ready",
                             "place_mm", "onehot_ready", "list_mm", "meta_ready"))
        gate_mm, up_mm, hidT_mm, down_mm, gath_mm, wselT_mm, scat_mm = (
            sem(n) for n in ("gate_mm", "up_mm", "hidT_mm", "down_mm", "gath_mm", "wselT_mm", "scat_mm"))
        gate_ready, up_ready, part_ready, hid_ready, pick_ready, sel_ready, wsel_ready, xg_ready = (
            sem(n) for n in ("gate_ready", "up_ready", "part_ready", "hid_ready", "pick_ready", "sel_ready",
                             "wsel_ready", "xg_ready"))
        sig_ready, hidT_ready, wselT_ready, yg_ready = (
            sem(n) for n in ("sig_ready", "hidT_ready", "wselT_ready", "yg_ready"))
        fsq_ready, fms_ready, fsd_ready, fin_ready = (sem(n) for n in ("fsq_ready", "fms_ready", "fsd_ready", "fin_ready"))
        o_slot = [sem(f"o_slot{m}") for m in range(3)]
        (o_sel, o_gath, o_xg, o_gate, o_up, o_gread, o_sig, o_hid, o_hidT_mm, o_hidT, o_wselT_mm, o_wselT,
         o_down, o_yg, o_scat) = (sem(f"o_{n}") for n in (
             "sel", "gath", "xg", "gate", "up", "gread", "sig", "hid", "hidT_mm", "hidT", "wselT_mm", "wselT",
             "down", "yg", "scat"))
        N_LIST = EXTRA * E

        def more_passes(eng, body):
            eng.wait_ge(meta_ready, 1)
            count = eng.value_load(meta[0:1, 2 * N_LIST:2 * N_LIST + 1], min_val=0, max_val=N_LIST)
            with eng.If(count > 0):
                with eng.Fori(0, count) as m:
                    body(m)
            return count

        def expert_of(eng, m):
            return eng.value_load(meta[0:1, bass.ds(m, 1)], min_val=0, max_val=E - 1)

        def place_of(eng, m):
            return eng.value_load(meta[0:1, bass.ds(m + N_LIST, 1)], min_val=CAP, max_val=CAP * EXTRA)

        block = ctx.enter_context(nc.Block())

        @block.sync
        def _(sp):
            sp.dma_start(xT, a["xT"].rearrange("(k p) t -> p k t", p=P)).then_inc(d_xT, 16)
            sp.dma_start(cols[:], a["cols"]).then_inc(d_cols, 16)
            for c in range(CC):
                sp.dma_start(w_conv[:, c], a["w_conv"][c]).then_inc(d_conv[c], 16)
            sp.dma_start(w_qk, a["w_qk"].rearrange("c p k n -> p c k n")).then_inc(d_qk, 16)
            sp.dma_start(w_v, a["w_v"]).then_inc(d_v, 16)
            sp.dma_start(relb, a["relb"]).then_inc(d_rel, 16)

            def load(kind, e, s, h):
                src = a[kind][bass.ds(e, 1)].rearrange("o (k p) n -> p (o k) n", p=P)
                n = KT // 2
                sp.dma_start(slot[:, s, h * n:(h + 1) * n], src[:, h * n:(h + 1) * n]).then_inc(d_slot[s][h], 16)

            for h in range(2):
                load("w_gate", 0, 0, h)
            sp.dma_start(router_w[:], a["router_w"].rearrange("(k p) e -> p k e", p=P)).then_inc(d_small, 16)
            sp.dma_start(router_b[:], a["router_b"]).then_inc(d_small, 16)
            sp.dma_start(bias_gu[:], a["bias_gu"]).then_inc(d_bias, 16)
            for h in range(2):
                load("w_up", 0, 1, h)
            sp.wait_ge(conv_mm, CC)
            sp.dma_start(w_out, a["w_out"].rearrange("(k p) n -> p k n", p=P)).then_inc(d_wout, 16)
            sp.wait_ge(v_mm, TT)
            sp.dma_start(x_tok, a["x"].rearrange("(t p) d -> p t d", p=P)).then_inc(d_xtok, 16)
            for h in range(2):
                load("w_gate", 1, 3, h)
            sp.wait_ge(cleared, 1)
            sp.dma_start(yg[0:E, 0], a["b_down"][:, 0:HB]).then_inc(d_yg, 16)
            sp.dma_start(yg[CAP:CAP + E, 1], a["b_down"][:, HB:D]).then_inc(d_yg, 16)
            sp.wait_ge(av_ready, HEADS // 2)
            sp.dma_start(gain_ffn, a["gain_ffn"]).then_inc(d_gffn, 16)
            sp.wait_ge(out_mm, 1)
            for h in range(2):
                load("w_down", 0, 2, h)
            for h in range(2):
                load("w_up", 1, 4, h)
            sp.wait_ge(meta_ready, 1)
            sp.dma_start(late[:], a["gain_last"]).then_inc(d_gfin, 16)

            with sp.Fori(0, PAIRS - 1) as i:
                n = i * 2
                sp.wait_ge(down_mm, n + 1)
                for h in range(2):
                    load("w_down", n + 1, 2, h)
                for h in range(2):
                    load("w_gate", n + 2, 0, h)
                for h in range(2):
                    load("w_up", n + 2, 1, h)
                sp.wait_ge(down_mm, n + 2)
                for h in range(2):
                    load("w_down", n + 2, 2, h)
                for h in range(2):
                    load("w_gate", n + 3, 3, h)
                for h in range(2):
                    load("w_up", n + 3, 4, h)
            sp.wait_ge(down_mm, E - 1)
            for h in range(2):
                load("w_down", E - 1, 2, h)

            def weights_again(m):
                e = expert_of(sp, m)
                sp.wait_ge(down_mm, E)
                sp.wait_ge(o_scat, m + 1)
                for k, kind in enumerate(("w_gate", "w_up", "w_down")):
                    src = a[kind][bass.ds(e, 1)].rearrange("o (k p) n -> p (o k) n", p=P)
                    sp.dma_start(slot[:, k], src).then_inc(o_slot[k], 16)

            more_passes(sp, weights_again)
            for t in range(TT):
                sp.wait_ge(fin_ready, t + 1)
                sp.dma_start(out.rearrange("(t p) d -> p t d", p=P)[:, t], outb[:, t]).then_inc(d_out, 16)
            sp.wait_ge(d_out, 16 * TT)

        @block.gpsimd
        def _(pool):
            g = nc.gpsimd
            st = Steps(pool, pool_step)

            def one(ins):
                st.mark(ins)
                st.wait()

            one(g.memset(ones[:], 1.0))
            one(g.memset(ident_w[:], 0.0))
            one(g.affine_select(out=ident, in_=ident, compare_op=ALU.not_equal, fill=1.0, base=0,
                                pattern=[[-1, P]], channel_multiplier=1))
            one(g.memset(before[:], 1.0))
            one(g.affine_select(out=before[:], in_=before[:], compare_op=ALU.is_gt, fill=0.0, base=0,
                                pattern=[[1, P]], channel_multiplier=-1))
            one(g.iota(iota[:], pattern=[[1, T]], base=0, channel_multiplier=0, allow_small_or_imprecise_dtypes=True))
            for c in range(EXTRA):
                q = slice(32 * c, 32 * c + 32)
                one(g.iota(code_e[q], pattern=[[0, 1]], base=0, channel_multiplier=1,
                           allow_small_or_imprecise_dtypes=True))
                one(g.memset(code_c[q], float(CAP * (c + 1))))
                one(g.memset(thresh[q], float(CAP * (c + 1))))
            one(g.memset(rank[:], -1.0))
            one(g.memset(share[:], 0.0))
            g.memset(padded[:, :, 0:PAD], 0.0).then_inc(const_ready, 1)
            pool.wait_ge(const_ready, 1)
            pool.wait_ge(conv_ready, CC)
            g.memset(yg, 0.0).then_inc(cleared, 1)

        @block.scalar
        def _(act):
            s = nc.scalar
            act.wait_ge(d_xT, 16)
            for h in range(2):
                s.activation(xsq[:, 4 * h:4 * h + 4], xT[:, 4 * h:4 * h + 4], ACT.Square).then_inc(sq_ready, 1)
            act.wait_ge(var_ready, 1)
            s.activation(rstd_row, rstd_row, ACT.Sqrt).then_inc(sd_ready, 1)
            for c in range(CC):
                act.wait_ge(conv_mm, c + 1)
                s.activation(sgate[:, c], bank[c][:, T:2 * T], ACT.Sigmoid).then_inc(sgate_ready, 1)
            for c in range(4):
                act.wait_ge(qk_mm, c + 1)
                s.activation(qkT[:, c].rearrange("p w t -> p (w t)"), y[:, c], ACT.Copy).then_inc(qk_ready, 1)
            for t in range(TT):
                act.wait_ge(v_mm, t + 1)
                s.activation(val[:, t], bank[t][:], ACT.Copy).then_inc(v_ready, 1)
            act.wait_ge(cent_ready, 1)
            s.activation(lnsq, acc, ACT.Square).then_inc(lnsq_ready, 1)
            act.wait_ge(lnv_ready, 1)
            s.activation(lnrow[:, 0], lnrow[:, 0], ACT.Sqrt).then_inc(lnsd_ready, 1)
            for c in range(CC):
                act.wait_ge(xn_ready, c + 1)
                s.activation(padded[:, c, 0:T], acc[:, c], ACT.Sigmoid, bias=ln_b[:, c:c + 1],
                             scale=ln_g[:, c:c + 1]).then_inc(lnsig_ready, 1)
            for h in range(HEADS + 1):
                if h < HEADS:
                    p, q = h % 2, 2 * (h % 2)
                    act.wait_ge(max_ready, h + 1)
                    s.activation(probs[:, p, 0:T], probs[:, p, 0:T], ACT.Exp, bias=negmax[:, q:q + 1],
                                 accum_out=den[:, q:q + 1])
                    s.activation(probs[:, p, T:3 * P], probs[:, p, T:3 * P], ACT.Exp, bias=negmax[:, q + 1:q + 2],
                                 accum_out=den[:, q + 1:q + 2]).then_inc(exp_ready, 1)
                if h >= 1:
                    act.wait_ge(probsT_mm, h)
                    s.activation(probsT[:, (h - 1) % 2], b6[:, 0:3 * P], ACT.Copy).then_inc(probsT_ready, 1)
                    if h % 2 == 0:
                        c = h // 2 - 1
                        act.wait_ge(av_mm, h)
                        s.activation(mixT[:, c], b7[:, (c % 2) * T:(c % 2 + 1) * T], ACT.Copy).then_inc(av_ready, 1)
            act.wait_ge(out_mm, 1)
            for t in range(TT):
                s.activation(mixT[:, 4 * t:4 * t + 4].rearrange("p c t -> p (c t)"), y[:, 2 * t:2 * t + 2].rearrange("p h n -> p (h n)"), ACT.Square,
                             accum_out=ssq[:, t:t + 1]).then_inc(ssq_ready, 1)
            act.wait_ge(ms_ready, 1)
            s.activation(rstd, rstd, ACT.Sqrt).then_inc(rms_sd, 1)
            for t in range(TT):
                act.wait_ge(h2T_mm, 2 * t + 1)
                s.activation(hT[:, 0:4, t * P:(t + 1) * P], bank[2 * t][:].rearrange("p (k n) -> p k n", k=4),
                             ACT.Copy).then_inc(h2T_act, 1)
            act.wait_ge(top_shift, 1)
            s.activation(topw, topw, ACT.Exp).then_inc(top_exp, 1)
            act.wait_ge(wselT_mm, 1)
            s.activation(wselT.rearrange("p o t -> p (o t)"), b5[:], ACT.Copy).then_inc(wselT_ready, 1)

            with act.Fori(0, PAIRS) as i:
                for j in range(2):
                    n = i * 2 + j
                    act.wait_ge(gate_ready, n + 1)
                    s.activation(sig, gate, ACT.Sigmoid, scale=ALPHA).then_inc(sig_ready, 1)
                    act.wait_ge(hidT_mm, n + 1)
                    s.activation(hidT.rearrange("p a b -> p (a b)"), b5[:], ACT.Copy).then_inc(hidT_ready, 1)
                act.wait_ge(down_mm, i * 2 + 2)
                s.activation(yg[:, 0], b6[:], ACT.Copy)
                s.activation(yg[:, 1], b7[:], ACT.Copy).then_inc(yg_ready, 1)
                act.wait_ge(wselT_mm, i + 2)
                s.activation(wselT.rearrange("p o t -> p (o t)"), b5[:], ACT.Copy).then_inc(wselT_ready, 1)

            def again(m):
                act.wait_ge(o_wselT_mm, m + 1)
                s.activation(wselT.rearrange("p o t -> p (o t)"), b7[:], ACT.Copy).then_inc(o_wselT, 1)
                act.wait_ge(o_gread, m + 1)
                s.activation(sig, gate, ACT.Sigmoid, scale=ALPHA).then_inc(o_sig, 1)
                act.wait_ge(o_hidT_mm, m + 1)
                s.activation(hidT.rearrange("p a b -> p (a b)"), b5[:], ACT.Copy).then_inc(o_hidT, 1)
                act.wait_ge(o_down, m + 1)
                s.activation(yg[0:CAP, 0], b6[0:CAP], ACT.Copy)
                s.activation(yg[CAP:P, 1], b7[CAP:P], ACT.Copy).then_inc(o_yg, 1)

            count = more_passes(act, again)
            act.wait_ge(o_scat, count + 1)
            for t in range(TT):
                s.activation(slot[:, 1, t], y[:, 2 * t:2 * t + 2].rearrange("p h n -> p (h n)"), ACT.Square,
                             accum_out=fsq[:, t:t + 1]).then_inc(fsq_ready, 1)
            act.wait_ge(fms_ready, 1)
            s.activation(frstd, frstd, ACT.Sqrt).then_inc(fsd_ready, 1)

        @block.vector
        def _(dve):
            v = nc.vector
            st = Steps(dve, dve_step)
            dve.wait_ge(ssum_done, 1)
            v.tensor_scalar(rstd_row, y[:, 0, 0:T], 1.0 / D, EPS, ALU.mult, ALU.add).then_inc(var_ready, 1)
            dve.wait_ge(sd_ready, 1)
            st.mark(v.reciprocal(rstd_row, rstd_row))
            dve.wait_ge(d_cols, 16)
            st.wait()
            for k in range(KT):
                v.scalar_tensor_tensor(out=hT[:, k], in0=xT[:, k], scalar=g_mix[:, k:k + 1], in1=rstd_row,
                                       op0=ALU.mult, op1=ALU.mult).then_inc(hT_ready, 1)
            dve.wait_ge(const_ready, 1)
            last = [0] * CC
            for c in range(CC):
                dve.wait_ge(sgate_ready, c + 1)
                ins = v.tensor_tensor(padded[:, c, PAD:PAD + T], bank[c][:, 0:T], sgate[:, c], ALU.mult)
                ins.then_inc(conv_read, 1)
                if c % 2 == 0:
                    continue
                dve.wait_ge(conv_read, c + 1)
                for k in range(TAPS):
                    for cc in (c - 1, c):
                        if k == 0:
                            ins = v.tensor_scalar(acc[:, cc], padded[:, cc, 0:T], dw[:, cc, 0:1], dw_b[:, cc:cc + 1],
                                                  ALU.mult, ALU.add)
                        else:
                            st.wait(last[cc])
                            ins = v.scalar_tensor_tensor(out=acc[:, cc], in0=padded[:, cc, k:k + T],
                                                         scalar=dw[:, cc, k:k + 1], in1=acc[:, cc],
                                                         op0=ALU.mult, op1=ALU.add)
                        if k < TAPS - 1:
                            last[cc] = st.mark(ins)
                        else:
                            ins.then_inc(acc_ready, 1)
            dve.wait_ge(acc_ready, CC)
            dve.wait_ge(mu_mm, 1)
            for c in range(CC):
                ins = v.scalar_tensor_tensor(out=acc[:, c], in0=b6[:, 0:T], scalar=-1.0 / D_CONV, in1=acc[:, c],
                                             op0=ALU.mult, op1=ALU.add)
            ins.then_inc(cent_ready, 1)
            dve.wait_ge(lnv_mm, 1)
            v.tensor_scalar(lnrow[:, 0], b7[:, 0:T], 1.0 / D_CONV, EPS, ALU.mult, ALU.add).then_inc(lnv_ready, 1)
            dve.wait_ge(lnsd_ready, 1)
            st.mark(v.reciprocal(lnrow[:, 0], lnrow[:, 0]))
            st.wait()
            dve.wait_ge(cent_ready, 1)
            for c in range(CC):
                v.tensor_tensor(acc[:, c], acc[:, c], lnrow[:, 0], ALU.mult).then_inc(xn_ready, 1)
            for c in range(CC):
                dve.wait_ge(xn_ready, c + 1)
                dve.wait_ge(lnsig_ready, c + 1)
                n = st.mark(v.tensor_scalar(acc[:, c], acc[:, c], ln_g[:, c:c + 1], ln_b[:, c:c + 1],
                                            ALU.mult, ALU.add))
                st.wait(n)
                v.tensor_tensor(mixT[:, CC + c], acc[:, c], padded[:, c, 0:T], ALU.mult).then_inc(conv_ready, 1)
            dve.wait_ge(d_rel, 16)
            st.mark(v.memset(relb[0:64, :, T - 64:T], MASKED))
            st.wait()

            def softmax_in(h):
                p, q = h % 2, 2 * (h % 2)
                dve.wait_ge(score_mm, h + 1)
                if h >= 2:
                    dve.wait_ge(probsT_mm, h - 1)
                v.scalar_tensor_tensor(out=probs[:, p, 0:T], in0=bank[p][:, 0:T], scalar=HD ** -0.5,
                                       in1=relb[:, h], op0=ALU.mult, op1=ALU.add)
                v.scalar_tensor_tensor(out=probs[:, p, T:3 * P], in0=bank[p][:, T:3 * P], scalar=HD ** -0.5,
                                       in1=relb[:, h, P:T], op0=ALU.mult, op1=ALU.add).then_inc(score_read, 1)
                dve.wait_ge(score_read, h + 1)
                v.tensor_reduce(negmax[:, q:q + 1], probs[:, p, 0:T], AX.X, ALU.max, negate=True)
                v.tensor_reduce(negmax[:, q + 1:q + 2], probs[:, p, T:3 * P], AX.X, ALU.max,
                                negate=True).then_inc(max_ready, 1)

            def softmax_out(h):
                p, q = h % 2, 2 * (h % 2)
                dve.wait_ge(exp_ready, h + 1)
                st.mark(v.reciprocal(rden[:, q:q + 2], den[:, q:q + 2]))
                st.wait()
                v.tensor_scalar(probs[:, p, 0:T], probs[:, p, 0:T], rden[:, q:q + 1], None, ALU.mult)
                v.tensor_scalar(probs[:, p, T:3 * P], probs[:, p, T:3 * P], rden[:, q + 1:q + 2], None,
                                ALU.mult).then_inc(probs_ready, 1)

            for h in range(HEADS + 1):
                if h < HEADS:
                    softmax_in(h)
                if h >= 1:
                    softmax_out(h - 1)
            dve.wait_ge(ssq_ready, TT)
            v.tensor_scalar(rstd, ssq, 1.0 / D, EPS, ALU.mult, ALU.add).then_inc(ms_ready, 1)
            dve.wait_ge(rms_sd, 1)
            st.mark(v.reciprocal(rstd, rstd))
            st.wait()
            dve.wait_ge(d_gffn, 16)
            for t in range(TT):
                v.scalar_tensor_tensor(out=h2[:, t], in0=y[:, 2 * t:2 * t + 2].rearrange("p h n -> p (h n)"),
                                       scalar=rstd[:, t:t + 1], in1=gain_ffn, op0=ALU.mult,
                                       op1=ALU.mult).then_inc(h2_ready, 1)
            for t in range(TT):
                dve.wait_ge(h2T_mm, 2 * t + 2)
                v.tensor_copy(hT[:, 4:8, t * P:(t + 1) * P],
                              bank[2 * t + 1][:].rearrange("p (k n) -> p k n", k=4)).then_inc(h2T_dve, 1)
            dve.wait_ge(lg_mm, 1)
            v.tensor_copy(lgT, b4[:, 0:T]).then_inc(lgT_ready, 1)
            dve.wait_ge(lgt_mm, 1)
            st.mark(v.tensor_reduce(lg, b5[:, 0:T].rearrange("p (t q e) -> p t e q", t=TT, q=4), AX.X, ALU.add))
            st.wait()
            dve.wait_ge(d_small, 32)
            st.mark(v.tensor_tensor(lg, lg, router_b[:].unsqueeze(1).to_broadcast([P, TT, E]), ALU.add))
            st.wait()
            for t in range(TT):
                ins = v.max(topv[:, t], lg[:, t])
            st.mark(ins)
            st.wait()
            for t in range(TT):
                v.max_index(topi[:, t], topv[:, t], lg[:, t])
            v.tensor_tensor(topw, topv[:, :, 0:TOPK], topv[:, :, 0:1].to_broadcast([P, TT, TOPK]),
                            ALU.subtract).then_inc(top_shift, 1)
            dve.wait_ge(top_shift, 1)
            st.mark(v.tensor_copy(topf, topi[:, :, 0:TOPK]))
            st.wait()
            st.mark(v.tensor_tensor(hit.rearrange("p (t k) e -> p t k e", t=TT),
                                    iota[:, 0:E].unsqueeze(1).unsqueeze(1).to_broadcast([P, TT, TOPK, E]),
                                    topf.unsqueeze(3).to_broadcast([P, TT, TOPK, E]), ALU.is_equal))
            st.wait()
            v.tensor_reduce(mask, hit.rearrange("p (t k) e -> p t e k", t=TT), AX.X, ALU.add).then_inc(mask_ready, 1)
            dve.wait_ge(mask_ready, 1)
            v.tensor_copy(mask3.rearrange("p t (c e) -> p t c e", c=EXTRA),
                          mask.unsqueeze(2).to_broadcast([P, TT, EXTRA, E])).then_inc(mask_ready, 1)
            dve.wait_ge(top_exp, 1)
            st.mark(v.tensor_reduce(wsum, topw, AX.X, ALU.add))
            st.wait()
            st.mark(v.reciprocal(wsum, wsum))
            st.wait()
            st.mark(v.tensor_tensor(topw, topw, wsum.unsqueeze(2).to_broadcast([P, TT, TOPK]), ALU.mult))
            st.wait()
            st.mark(v.tensor_tensor(whit.rearrange("p (t k) e -> p t k e", t=TT),
                                    hit.rearrange("p (t k) e -> p t k e", t=TT),
                                    topw.unsqueeze(3).to_broadcast([P, TT, TOPK, E]), ALU.mult))
            st.wait()
            st.mark(v.tensor_reduce(share[:, :, 0:E], whit.rearrange("p (t k) e -> p t e k", t=TT), AX.X, ALU.add))
            dve.wait_ge(rank_mm, 1)
            st.mark(v.scalar_tensor_tensor(out=rank[:, :, 0:E], in0=b6[:, 0:TT * E].rearrange("p (t e) -> p t e", t=TT),
                                           scalar=1.0, in1=mask, op0=ALU.add, op1=ALU.mult))
            st.wait()
            st.mark(v.tensor_scalar(rank[:, :, 0:E], rank[:, :, 0:E], -1.0, None, ALU.add))
            st.wait()

            def build_sel(e, places, width):
                k = width // CAP
                return v.tensor_tensor(
                    sel[:, :, 0:width].rearrange("p t (k c) -> p t k c", k=k),
                    places.unsqueeze(1).unsqueeze(1).to_broadcast([P, TT, k, CAP]),
                    rank[:, :, bass.ds(e, k)].unsqueeze(3).to_broadcast([P, TT, k, CAP]), ALU.is_equal)

            def build_wsel(e, k):
                v.tensor_tensor(wsel[:, :, 0:k * CAP].rearrange("p t (k c) -> p t k c", k=k),
                                sel[:, :, 0:k * CAP].rearrange("p t (k c) -> p t k c", k=k),
                                share[:, :, bass.ds(e, k)].unsqueeze(3).to_broadcast([P, TT, k, CAP]), ALU.mult)
                return v.tensor_tensor(wsel[:, :, 2 * CAP:3 * CAP], sel[:, :, 0:CAP],
                                       share[:, :, bass.ds(e, 1)].to_broadcast([P, TT, CAP]), ALU.mult)

            def build_pick(e, j):
                src = ident_w[:, bass.ds(e, 4, E)]
                return v.tensor_copy(pick[:, j], src.unsqueeze(2).to_broadcast([P, 4, CAP]))

            build_sel(0, iota[:, 0:CAP], 2 * CAP).then_inc(sel_ready, 1)
            st.mark(v.memset(wsel, 0.0))
            st.wait()
            v.tensor_copy(wsel[:, :, 0:E], share[:, :, 0:E])
            v.tensor_copy(wsel[:, :, 2 * CAP:2 * CAP + E], share[:, :, 0:E]).then_inc(wsel_ready, 1)
            for j in range(2):
                ins = build_pick(j, j)
            ins.then_inc(pick_ready, 1)
            for k in range(2):
                dve.wait_ge(gath_mm, k + 1)
                v.tensor_copy(xg[:, 4 * k:4 * k + 4].rearrange("p a b -> p (a b)"),
                              bank[2 * k][:]).then_inc(xg_ready, 1)
            dve.wait_ge(cnt_mm, 1)
            v.tensor_scalar(flag[0:N_LIST], b7[0:N_LIST, 0:1], thresh[0:N_LIST], None, ALU.is_gt).then_inc(flag_ready, 1)
            dve.wait_ge(place_mm, 1)
            v.tensor_scalar(onehot[0:N_LIST], iota[0:N_LIST, 0:N_LIST], b7[0:N_LIST, 1:2], flag[0:N_LIST],
                            ALU.is_equal, ALU.mult).then_inc(onehot_ready, 1)
            dve.wait_ge(list_mm, 1)
            v.tensor_copy(meta[0:1, 0:2 * N_LIST + 1], b7[0:1, 8:8 + 2 * N_LIST + 1]).then_inc(meta_ready, 1)

            with dve.Fori(0, PAIRS) as i:
                dve.wait_ge(wselT_mm, i + 1)
                dve.wait_ge(sel_ready, i + 1)
                build_wsel(i * 2, 2).then_inc(wsel_ready, 1)
                for j in range(2):
                    n = i * 2 + j
                    dve.wait_ge(gate_mm, n + 1)
                    v.tensor_scalar(gate, b4[:], LIMIT, None, ALU.min).then_inc(gate_ready, 1)
                    if j == 0:
                        dve.wait_ge(wsel_ready, i + 2)
                        build_sel(i * 2 + 2, iota[:, 0:CAP], 2 * CAP).then_inc(sel_ready, 1)
                    dve.wait_ge(sig_ready, n + 1)
                    v.tensor_tensor(sig, gate, sig, ALU.mult).then_inc(part_ready, 1)
                    dve.wait_ge(up_mm, n + 1)
                    v.tensor_scalar(up, b5[:], LIMIT, -LIMIT, ALU.min, ALU.max).then_inc(up_ready, 1)
                    dve.wait_ge(part_ready, n + 1)
                    dve.wait_ge(up_ready, n + 1)
                    v.scalar_tensor_tensor(out=hid, in0=up, scalar=1.0, in1=sig, op0=ALU.add,
                                           op1=ALU.mult).then_inc(hid_ready, 1)
                for k in range(2):
                    dve.wait_ge(gath_mm, i * 2 + 3 + k)
                    v.tensor_copy(xg[:, 4 * k:4 * k + 4].rearrange("p a b -> p (a b)"), b4[:]).then_inc(xg_ready, 1)
                for j in range(2):
                    ins = build_pick(i * 2 + 2 + j, j)
                ins.then_inc(pick_ready, 1)

            def again(m):
                e = expert_of(dve, m)
                first = place_of(dve, m)
                dve.wait_ge(o_scat, m + 1)
                build_sel(e, iota[:, bass.ds(first, CAP)], CAP).then_inc(dve_over, 1)
                build_pick(e, 0)
                dve.wait_ge(dve_over, m + 1)
                build_wsel(e, 1).then_inc(o_sel, 1)
                dve.wait_ge(o_gath, m + 1)
                v.tensor_copy(xg[:, :, 0:CAP], b4[:].rearrange("p (k c) -> p k c", k=KT)).then_inc(o_xg, 1)
                dve.wait_ge(o_gate, m + 1)
                v.tensor_scalar(gate, b4[:], LIMIT, None, ALU.min).then_inc(o_gread, 1)
                dve.wait_ge(o_up, m + 1)
                v.tensor_scalar(up, b5[:], LIMIT, -LIMIT, ALU.min, ALU.max)
                dve.wait_ge(o_sig, m + 1)
                v.tensor_tensor(sig, gate, sig, ALU.mult).then_inc(dve_tail, 1)
                dve.wait_ge(dve_tail, m + 1)
                v.scalar_tensor_tensor(out=hid, in0=up, scalar=1.0, in1=sig, op0=ALU.add,
                                       op1=ALU.mult).then_inc(o_hid, 1)

            count = more_passes(dve, again)
            dve.wait_ge(o_scat, count + 1)
            dve.wait_ge(d_gfin, 16)
            dve.wait_ge(fsq_ready, TT)
            v.tensor_scalar(frstd, fsq, 1.0 / D, EPS, ALU.mult, ALU.add).then_inc(fms_ready, 1)
            dve.wait_ge(fsd_ready, 1)
            st.mark(v.reciprocal(frstd, frstd))
            st.wait()
            for t in range(TT):
                v.scalar_tensor_tensor(out=outb[:, t], in0=y[:, 2 * t:2 * t + 2].rearrange("p h n -> p (h n)"),
                                       scalar=frstd[:, t:t + 1], in1=late[:], op0=ALU.mult,
                                       op1=ALU.mult).then_inc(fin_ready, 1)

        @block.tensor
        def _(pe):
            def mm(o, l, r, start, stop=False, **kw):
                return pe.matmul(o, l, r, start=start, stop=stop, skip_group_check=True, **kw)

            pe.wait_ge(const_ready, 1)
            for k in range(KT):
                if k % 4 == 0:
                    pe.wait_ge(sq_ready, k // 4 + 1)
                last = mm(y[:, 0, 0:T], ones[:], xsq[:, k], k == 0, k == KT - 1)
            last.then_inc(ssum_done, 1)
            for c in range(CC):
                pe.wait_ge(d_conv[c], 16)
                for w in range(2):
                    for k in range(KT):
                        if c == 0 and w == 0:
                            pe.wait_ge(hT_ready, k + 1)
                        last = mm(bank[c][:, w * T:(w + 1) * T], w_conv[:, c, k, w * P:(w + 1) * P], hT[:, k],
                                  k == 0, k == KT - 1)
                last.then_inc(conv_mm, 1)
            pe.wait_ge(d_qk, 16)
            for c in range(4):
                for w in range(2):
                    for k in range(KT):
                        last = mm(y[:, c, w * T:(w + 1) * T], w_qk[:, c, k, w * P:(w + 1) * P], hT[:, k],
                                  k == 0, k == KT - 1)
                last.then_inc(qk_mm, 1)
            pe.wait_ge(d_v, 16)
            for t in range(TT):
                pe.wait_ge(conv_read, t + 1)
                for k in range(KT):
                    last = mm(bank[t][:], hT[:, k, t * P:(t + 1) * P], w_v[:, k], k == 0, k == KT - 1)
                last.then_inc(v_mm, 1)

            def scores(h):
                c, lo, b = h // 2, (h % 2) * HD, bank[h % 2]
                r = slice(lo, lo + HD)
                if h < 2:
                    pe.wait_ge(qk_ready, 4 if h else 1)
                    pe.wait_ge(v_ready, h + 1)
                else:
                    pe.wait_ge(score_read, h - 1)
                mm(b[:, 0:T], qkT[r, c, 0, P:T], qkT[r, c, 1, 0:T], True, True)
                mm(b[:, T:3 * P], qkT[r, c, 0, 0:P], qkT[r, c, 1, 0:P], True, True).then_inc(score_mm, 1)

            scores(0)
            scores(1)
            pe.wait_ge(acc_ready, CC)
            pe.wait_ge(conv_read, CC)
            for c in range(CC):
                last = mm(b6[:, 0:T], ones[:], acc[:, c], c == 0, c == CC - 1)
            last.then_inc(mu_mm, 1)
            pe.wait_ge(lnsq_ready, 1)
            for c in range(CC):
                last = mm(b7[:, 0:T], ones[:], lnsq[:, c], c == 0, c == CC - 1)
            last.then_inc(lnv_mm, 1)

            def out_part(k, t, h):
                o = y[:, 2 * t + h]
                if k is None:
                    return mm(o, ident, x_tok[:, t, h * HB:(h + 1) * HB], True)
                return mm(o, mixT[:, k, t * P:(t + 1) * P], w_out[:, k, h * HB:(h + 1) * HB], False)

            early = [(k, t, h) for k in (None, 4, 5, 6, 7) for t in range(TT) for h in range(2)]
            done = 0
            for h in range(HEADS):
                pe.wait_ge(probs_ready, h + 1)
                if h >= 1:
                    pe.wait_ge(probsT_ready, h)
                else:
                    pe.wait_ge(cent_ready, 1)
                p = h % 2
                for o, i in ((0, T), (P, 0), (T, P)):
                    last = pe.transpose(b6[:, o:o + P], probs[:, p, i:i + P], ident)
                last.then_inc(probsT_mm, 1)
                if h + 2 < HEADS:
                    scores(h + 2)
                if h == 0:
                    pe.wait_ge(qk_ready, 4)
                    pe.wait_ge(d_xtok, 16)
                while done < len(early) * (h + 1) // HEADS:
                    if done == 4:
                        pe.wait_ge(conv_ready, CC)
                        pe.wait_ge(d_wout, 16)
                    out_part(*early[done])
                    done += 1
                pe.wait_ge(probsT_ready, h + 1)
                c = h // 2
                if h == 0:
                    pe.wait_ge(lnv_ready, 1)
                if h % 2 == 0 and c >= 2:
                    pe.wait_ge(av_ready, c - 1)
                r, at = slice(p * HD, p * HD + HD), (c % 2) * T
                mm(b7[r, at:at + T], val[:, 0, h * HD:(h + 1) * HD], probsT[:, p, 0:T], True)
                mm(b7[r, at + P:at + T], val[:, 1, h * HD:(h + 1) * HD], probsT[:, p, T:3 * P], False,
                   True).then_inc(av_mm, 1)
            for k in range(4):
                pe.wait_ge(av_ready, k + 1)
                for t in range(TT):
                    for h in range(2):
                        last = out_part(k, t, h)
            last.then_inc(out_mm, 1)

            for t in range(TT):
                pe.wait_ge(h2_ready, t + 1)
                for k in range(KT):
                    last = pe.transpose(bank[2 * t + k // 4][:, (k % 4) * P:(k % 4 + 1) * P],
                                        h2[:, t, k * P:(k + 1) * P], ident)
                    if k % 4 == 3:
                        last.then_inc(h2T_mm, 1)
            pe.wait_ge(h2T_act, TT)
            pe.wait_ge(h2T_dve, TT)
            pe.wait_ge(d_small, 32)
            for r in range(2):
                for q in range(4):
                    k = 4 * r + q
                    last = mm(b4[32 * q:32 * q + 32, 0:T], router_w[:, k], hT[:, k], r == 0, r == 1)
            last.then_inc(lg_mm, 1)
            pe.wait_ge(lgT_ready, 1)
            for t in range(TT):
                last = pe.transpose(b5[:, t * P:(t + 1) * P], lgT[:, t * P:(t + 1) * P], ident)
            last.then_inc(lgt_mm, 1)
            pe.wait_ge(mask_ready, 1)
            mm(b6[:, 0:E], before[:], mask[:, 0], True, True)
            mm(b6[:, E:2 * E], ones[:], mask[:, 0], True)
            mm(b6[:, E:2 * E], before[:], mask[:, 1], False, True).then_inc(rank_mm, 1)

            def gather(k, o, width):
                n = HB // width
                for kk in range(n):
                    for t in range(TT):
                        f = (k + kk) * P
                        last = mm(o[:, kk * width:(kk + 1) * width], h2[:, t, f:f + P], sel[:, t, 0:width],
                                  t == 0, t == TT - 1)
                return last

            def weigh_T(o):
                for order in range(2):
                    for t in range(TT):
                        at = (order * TT + t) * P
                        last = pe.transpose(o[:, at:at + P], wsel[:, t, order * CAP:order * CAP + P], ident)
                return last

            def project(o, lhs, w, bias, j):
                if bias is not None:
                    for h in range(2):
                        mm(o[h * CAP:(h + 1) * CAP, :], pick[:, j, bias + h], bias_gu[:], True)
                for k in range(KT):
                    if k in w[1]:
                        pe.wait_ge(*w[1][k])
                    for h in range(2):
                        last = mm(o[h * CAP:(h + 1) * CAP, :], lhs(k), w[0][:, k, h * HB:(h + 1) * HB], False,
                                  k == KT - 1)
                return last

            def down(outs, w, j):
                for k in range(KT):
                    if k in w[1]:
                        pe.wait_ge(*w[1][k])
                    for h in range(2):
                        q = h ^ j
                        last = mm(outs[h][q * CAP:(q + 1) * CAP, :], hidT[:, k % 4, (k // 4) * CAP:(k // 4 + 1) * CAP],
                                  w[0][:, k, h * HB:(h + 1) * HB], k == 0, k == KT - 1)
                return last

            def hid_T(o):
                for c in range(4):
                    last = pe.transpose(o[:, c * P:(c + 1) * P], hid[:, c * P:(c + 1) * P], ident)
                return last

            def scatter(h, ts, rows=slice(0, P)):
                for t in ts:
                    last = mm(y[:, 2 * t + h], wselT[rows, h, t * P:(t + 1) * P], yg[rows, h], False)
                return last

            pe.wait_ge(sel_ready, 1)
            gather(0, b4, 2 * CAP).then_inc(gath_mm, 1)
            gather(4, b6, 2 * CAP).then_inc(gath_mm, 1)
            pe.wait_ge(wsel_ready, 1)
            weigh_T(b5).then_inc(wselT_mm, 1)
            pe.wait_ge(mask_ready, 2)
            for t in range(TT):
                last = mm(b7[0:N_LIST, 0:1], mask3[:, t], ones[:, 0:1], t == 0, t == TT - 1)
            last.then_inc(cnt_mm, 1)
            pe.wait_ge(flag_ready, 1)
            mm(b7[0:N_LIST, 1:2], before[0:N_LIST, 0:N_LIST], flag[0:N_LIST], True, True).then_inc(place_mm, 1)
            pe.wait_ge(onehot_ready, 1)
            mm(b7[0:1, 8:8 + N_LIST], code_e[0:N_LIST], onehot[0:N_LIST], True, True)
            mm(b7[0:1, 8 + N_LIST:8 + 2 * N_LIST], code_c[0:N_LIST], onehot[0:N_LIST], True, True)
            mm(b7[0:1, 8 + 2 * N_LIST:9 + 2 * N_LIST], flag[0:N_LIST], ones[0:N_LIST, 0:1], True,
               True).then_inc(list_mm, 1)
            pe.wait_ge(d_bias, 16)
            pe.wait_ge(d_yg, 32)
            pe.wait_ge(meta_ready, 1)

            with pe.Fori(0, PAIRS) as i:
                for j in range(2):
                    n = i * 2 + j

                    def weights(slots, count):
                        sl = slots[j]
                        return slot[:, sl], {0: (d_slot[sl][0], 16 * count), KT // 2: (d_slot[sl][1], 16 * count)}

                    def tokens(k):
                        return xg[:, k, j * CAP:(j + 1) * CAP]

                    if j == 0:
                        pe.wait_ge(pick_ready, i + 1)
                        pe.wait_ge(xg_ready, i * 2 + 2)
                    project(b4, tokens, weights(GATE, i + 1), 0, j).then_inc(gate_mm, 1)
                    if j == 0:
                        pe.wait_ge(wselT_ready, i + 1)
                    project(b5, tokens, weights(UP, i + 1), 2, j).then_inc(up_mm, 1)
                    if j == 0:
                        scatter(0, range(TT))
                        pe.wait_ge(hid_ready, n + 1)
                        hid_T(b5).then_inc(hidT_mm, 1)
                        scatter(1, range(TT)).then_inc(scat_mm, 1)
                    else:
                        pe.wait_ge(sel_ready, i + 2)
                        pe.wait_ge(gate_ready, n + 1)
                        gather(0, b4, 2 * CAP).then_inc(gath_mm, 1)
                        pe.wait_ge(hid_ready, n + 1)
                        hid_T(b5).then_inc(hidT_mm, 1)
                        pe.wait_ge(xg_ready, i * 2 + 3)
                        gather(4, b4, 2 * CAP).then_inc(gath_mm, 1)
                    pe.wait_ge(hidT_ready, n + 1)
                    down((b6, b7), weights(DOWN, n + 1), j).then_inc(down_mm, 1)
                    if j == 1:
                        pe.wait_ge(wsel_ready, i + 2)
                        weigh_T(b5).then_inc(wselT_mm, 1)
            pe.wait_ge(wselT_ready, PAIRS + 1)
            pe.wait_ge(yg_ready, PAIRS)
            scatter(0, range(TT)).then_inc(scat_mm, 1)
            scatter(1, range(TT)).then_inc(o_scat, 1)

            def again(m):
                pe.wait_ge(o_sel, m + 1)
                gather(0, b4, CAP).then_inc(o_gath, 1)
                weigh_T(b7).then_inc(o_wselT_mm, 1)
                pe.wait_ge(o_xg, m + 1)
                lhs = lambda k: xg[:, k, 0:CAP]
                whole = lambda k: (slot[:, k], {0: (o_slot[k], (m + 1) * 16)})
                project(b4, lhs, whole(0), 0, 0).then_inc(o_gate, 1)
                project(b5, lhs, whole(1), 2, 0).then_inc(o_up, 1)
                pe.wait_ge(o_hid, m + 1)
                hid_T(b5).then_inc(o_hidT_mm, 1)
                pe.wait_ge(o_hidT, m + 1)
                pe.wait_ge(o_wselT, m + 1)
                down((b6, b7), whole(2), 0).then_inc(o_down, 1)
                pe.wait_ge(o_yg, m + 1)
                scatter(0, range(TT), slice(0, CAP))
                scatter(1, range(TT), slice(CAP, P)).then_inc(o_scat, 1)

            more_passes(pe, again)


_SHAPES = ["x", "xT", "cols", "w_conv", "w_qk", "w_v", "relb", "w_out", "gain_ffn", "router_w", "router_b", "bias_gu",
           "w_gate", "w_up", "w_down", "b_down", "gain_last"]


def _lay_out(x, norm_mix_g, w_in, conv_dw_w, conv_dw_b, conv_ln_g, conv_ln_b, rel_bias, w_out, norm_ffn_g, router_w,
             router_b, exp_w_gate, exp_b_gate, exp_w_up, exp_b_up, exp_w_down, exp_b_down, norm_final_g):
    import numpy as np

    def columns(v):
        return v.reshape(-1, P).T

    def rows(v):
        return np.ascontiguousarray(np.broadcast_to(v, (P, v.shape[-1])))

    w = w_in[0].reshape(KT, P, -1).transpose(1, 0, 2)
    q, k, v, conv, gate = (w[:, :, i * HB:(i + 1) * HB] for i in range(5))

    def pairs(l, r):
        return np.ascontiguousarray(np.stack(
            [np.concatenate([l[:, :, c * P:(c + 1) * P], r[:, :, c * P:(c + 1) * P]], axis=2) for c in range(4)]))

    back = rel_bias[0][:, ::-1]
    ext = np.concatenate([np.repeat(back[:, :1], P - 1, axis=1), back, np.repeat(back[:, -1:], 64, axis=1)], axis=1)
    relb = np.stack([ext[:, P - 1 - p:P - 1 - p + T] for p in range(P)])
    taps = conv_dw_w[0].T.reshape(CC, P, TAPS).transpose(1, 0, 2).reshape(P, CC * TAPS)
    bg, bu = exp_b_gate[0], exp_b_up[0]
    return {
        "x": x[0], "xT": x[0].T,
        "cols": np.concatenate([columns(norm_mix_g[0]), taps, columns(conv_dw_b[0]), columns(conv_ln_g[0]),
                                columns(conv_ln_b[0])], axis=1),
        "w_conv": pairs(conv, gate), "w_qk": pairs(q, k), "w_v": v, "relb": relb, "w_out": w_out[0],
        "gain_ffn": rows(norm_ffn_g[0]), "router_w": router_w[0], "router_b": rows(router_b[0]),
        "bias_gu": np.concatenate([bg[:, :HB], bg[:, HB:], bu[:, :HB], bu[:, HB:]], axis=0),
        "w_gate": exp_w_gate[0], "w_up": exp_w_up[0], "w_down": exp_w_down[0], "b_down": exp_b_down[0],
        "gain_last": rows(norm_final_g),
    }


def kernel(**inputs):
    import numpy as np
    import concourse.bacc as bacc
    from concourse.bass_utils import run_bass_kernel_spmd

    laid = _lay_out(**{k: np.asarray(v) for k, v in inputs.items()})
    nc = bacc.Bacc("TRN2", target_bir_lowering=False, num_devices=1)
    arrays, args = {}, {}
    for name in _SHAPES:
        v = np.ascontiguousarray(laid[name])
        arrays[f"in_{name}"] = v
        args[name] = nc.dram_tensor(f"in_{name}", v.shape, mybir.dt.from_np(v.dtype), kind="ExternalInput").ap()
    out = nc.dram_tensor("out_y", (T, D), F32, kind="ExternalOutput").ap()
    build_block(nc, args, out)
    r = run_bass_kernel_spmd(nc, [arrays], core_ids=[0])
    return r.results[0]["out_y"].reshape(1, T, D)
```

```python
from contextlib import ExitStack

import concourse.bass as bass
from concourse import mybir

P = 128
F32 = mybir.dt.float32
I32 = mybir.dt.int32
U32 = mybir.dt.uint32
ALU = mybir.AluOpType
ACT = mybir.ActivationFunctionType
AX = mybir.AxisListType

D = 1024
T = 256
KT = D // P
TT = T // P
HEADS, HD = 8, 64
D_ATTN = HEADS * HD
D_CONV = 512
CC = D_CONV // P
TAPS = 31
PAD = TAPS - 1
E = 32
TOPK = 4
CAP = 64
EXTRA = T // CAP - 1
PAIRS = E // 2
LIMIT = 7.0
ALPHA = 1.702
EPS = 1e-5
MASKED = -1e30
HB = 512


class Steps:

    def __init__(self, eng, sem):
        self.eng, self.sem, self.n = eng, sem, 0

    def mark(self, ins):
        ins.then_inc(self.sem, 1)
        self.n += 1
        return self.n

    def wait(self, n=None):
        self.eng.wait_ge(self.sem, self.n if n is None else n)


def build_block(nc, a, out):
    with ExitStack() as ctx:
        def sb(name, shape, dt=F32):
            return ctx.enter_context(nc.sbuf_tensor(name, shape, dt))

        def psum(name, shape):
            return ctx.enter_context(nc.psum_tensor(name, shape, F32))

        def sem(name):
            return ctx.enter_context(nc.semaphore(name))

        y = psum("y", [P, 2 * TT, HB])
        b4, b5, b6, b7 = (psum(f"b{i}", [P, HB]) for i in range(4, 8))
        bank = [b4, b5, b6, b7]

        slot = sb("slot", [P, 5, KT, D])
        GATE, UP, DOWN = (0, 3), (1, 4), (2, 2)
        work = sb("work", [P, 6392])
        h2 = sb("h2", [P, TT, D])
        late = sb("late", [P, D])
        probsT = sb("probsT", [P, 2, 3 * P])
        router_w = sb("router_w", [P, KT, E])
        router_b = sb("router_b", [P, E])
        ident_w = sb("ident_w", [P, P + 2])
        ident = ident_w[:, 0:P]
        ones = sb("ones", [P, P])
        before = sb("before", [P, P])
        iota = sb("iota", [P, T])
        bias_gu = sb("bias_gu", [P, HB])
        rank = sb("rank", [P, TT, E + 2])
        share = sb("share", [P, TT, E + 2])
        cols = sb("cols", [P, KT + CC * TAPS + 3 * CC])
        sm = sb("sm", [P, 64])
        meta = sb("meta", [1, 2 * EXTRA * E + 8], I32)

        def part(t, at, shape):
            n = 1
            for s in shape:
                n *= s
            v = t[:, at:at + n]
            if len(shape) == 1:
                return v
            names = "abc"[:len(shape)]
            return v.rearrange(f"p ({' '.join(names)}) -> p {' '.join(names)}",
                               **{c: s for c, s in zip(names[1:], shape[1:])})

        xg = part(work, 0, [KT, 2 * CAP])
        hid = part(work, 1024, [HB])
        hidT = part(work, 1536, [4, P])
        gate = part(work, 2048, [HB])
        up = part(work, 2560, [HB])
        yg = part(work, 3072, [2, HB])
        sel = part(work, 4216, [TT, 2 * CAP])
        wsel = part(work, 4472, [TT, 3 * CAP])
        wselT = part(work, 4856, [2, T])
        pick = part(work, 5368, [2, 4, CAP])
        sig = part(work, 5880, [HB])
        hT = part(work, 0, [KT, T])
        rstd_row = part(late, 768, [T])
        hT_flat = part(work, 0, [KT * T])
        val = part(work, 2048, [TT, D_ATTN])
        gain_ffn = part(work, 3072, [D])
        padded = part(work, 3072, [CC, PAD + T])
        lnsq = part(work, 3072, [CC, T])
        mixT = part(work, 4216, [2 * CC, T])
        xsq = part(work, 4216, [KT, T])
        h2f = h2[:].rearrange("p t d -> p (t d)")
        xT = part(h2f, 0, [KT, T])
        acc = part(h2f, 0, [CC, T])
        sgate = part(h2f, 1024, [CC, T])
        lnrow = part(h2f, 1024, [CC, T])
        probs = part(late, 0, [2, 3 * P])
        lgT = part(work, 2048, [T])
        lg = part(work, 2304, [TT, E])
        hit = part(work, 2368, [TT * TOPK, E])
        whit = part(work, 2624, [TT * TOPK, E])
        mask = part(work, 2880, [TT, E])
        mask3 = part(work, 2048, [TT, EXTRA * E])
        w_conv = slot[:, 4].rearrange("p a b -> p (a b)").rearrange("p (c k n) -> p c k n", c=CC, k=KT)
        w_qk = slot[:, 3].rearrange("p a b -> p (a b)").rearrange("p (c k n) -> p c k n", c=4, k=KT)
        w_out = slot[:, 4]
        s2 = slot[:, 2].rearrange("p a b -> p (a b)")
        w_v = s2[:, 0:4096].rearrange("p (k n) -> p k n", k=KT)
        qkT = s2[:, 4096:6144].rearrange("p (c w t) -> p c w t", c=4, w=2)
        relb = s2[:, 6144:8192].rearrange("p (h k) -> p h k", h=HEADS)
        outb = slot[:, 0].rearrange("p a b -> p (a b)")[:, 0:TT * D].rearrange("p (t d) -> p t d", t=TT)
        g_mix = cols[:, 0:KT]
        dw = cols[:, KT:KT + CC * TAPS].rearrange("p (c k) -> p c k", c=CC)
        c0 = KT + CC * TAPS
        dw_b, ln_g, ln_b = (cols[:, c0 + i * CC:c0 + (i + 1) * CC] for i in range(3))
        negmax, den, rden = sm[:, 0:4], sm[:, 4:8], sm[:, 8:12]
        ssq, rstd = sm[:, 16:20], sm[:, 14:16]
        fsq, frstd = sm[:, 16:18], sm[:, 18:20]
        topv = sm[:, 20:36].rearrange("p (t k) -> p t k", t=TT)
        topw = sm[:, 36:44].rearrange("p (t k) -> p t k", t=TT)
        topi = sb("topi", [P, TT, 8], U32)
        topf = sm[:, 44:52].rearrange("p (t k) -> p t k", t=TT)
        wsum = sm[:, 52:54]
        rstd_col = sm[:, 59:61]
        dummy = sm[0:1, 61:63]
        code_e, code_c, thresh, flag, place = (sm[:, 54 + i:55 + i] for i in range(5))
        onehot = part(work, 2048 + TT * EXTRA * E, [EXTRA * E])

        d_cols, d_qk, d_v, d_wout, d_rel, d_small, d_gffn, d_bias, d_yg, d_gfin, d_out = (
            sem(f"d_{n}") for n in ("cols", "qk", "v", "wout", "rel", "small", "gffn",
                                    "bias", "yg", "gfin", "out"))
        d_xT = [sem(f"d_xT{h}") for h in range(2)]
        d_conv = [sem(f"d_conv{c}") for c in range(CC + 1)]
        d_last = [sem(f"d_last{q}") for q in range(4)]
        d_slot = [[sem(f"d_slot{s}{h}") for h in range(2)] for s in range(5)]
        ident_ready, const_ready, cleared = sem("ident_ready"), sem("const_ready"), sem("cleared")
        norm_ready, col_mm, col_ready, gate_in, seed_mm = (
            sem(n) for n in ("norm_ready", "col_mm", "col_ready", "gate_in", "seed_mm"))
        pool_step, dve_step, act_step = sem("pool_step"), sem("dve_step"), sem("act_step")
        dve_tail, dve_over = sem("dve_tail"), sem("dve_over")
        sq_ready, ssum_done, var_ready, sd_ready = (sem(n) for n in ("sq_ready", "ssum_done", "var_ready", "sd_ready"))
        hT_ready, conv_mm, sgate_ready, conv_read = (sem(n) for n in ("hT_ready", "conv_mm", "sgate_ready", "conv_read"))
        qk_mm, qk_ready, v_mm, v_ready = (sem(n) for n in ("qk_mm", "qk_ready", "v_mm", "v_ready"))
        acc_ready, mu_mm, cent_ready, lnsq_ready, lnv_mm, lnv_ready, lnsd_ready, xn_ready, lnsig_ready, conv_ready = (
            sem(n) for n in ("acc_ready", "mu_mm", "cent_ready", "lnsq_ready", "lnv_mm", "lnv_ready",
                             "lnsd_ready", "xn_ready", "lnsig_ready", "conv_ready"))
        score_mm, score_read, max_ready, exp_ready, probs_ready, probsT_mm, probsT_ready, av_mm, av_ready = (
            sem(n) for n in ("score_mm", "score_read", "max_ready", "exp_ready", "probs_ready", "probsT_mm",
                             "probsT_ready", "av_mm", "av_ready"))
        out_mm, ssq_ready, ms_ready, rms_sd, h2_ready, h2T_mm, h2T_act, h2T_dve, lg_mm, lgT_ready, lgt_mm = (
            sem(n) for n in ("out_mm", "ssq_ready", "ms_ready", "rms_sd", "h2_ready", "h2T_mm", "h2T_act",
                             "h2T_dve", "lg_mm", "lgT_ready", "lgt_mm"))
        top_shift, top_exp, mask_ready, rank_mm, cnt_mm, flag_ready, place_mm, onehot_ready, list_mm, meta_ready = (
            sem(n) for n in ("top_shift", "top_exp", "mask_ready", "rank_mm", "cnt_mm", "flag_ready",
                             "place_mm", "onehot_ready", "list_mm", "meta_ready"))
        gate_mm, up_mm, hidT_mm, down_mm, gath_mm, wselT_mm, scat_mm = (
            sem(n) for n in ("gate_mm", "up_mm", "hidT_mm", "down_mm", "gath_mm", "wselT_mm", "scat_mm"))
        gate_ready, up_ready, part_ready, hid_ready, pick_ready, sel_ready, wsel_ready, xg_ready = (
            sem(n) for n in ("gate_ready", "up_ready", "part_ready", "hid_ready", "pick_ready", "sel_ready",
                             "wsel_ready", "xg_ready"))
        sig_ready, hidT_ready, wselT_ready, yg_ready = (
            sem(n) for n in ("sig_ready", "hidT_ready", "wselT_ready", "yg_ready"))
        fsq_ready, fms_ready, fsd_ready, fin_ready = (sem(n) for n in ("fsq_ready", "fms_ready", "fsd_ready", "fin_ready"))
        o_slot = [sem(f"o_slot{m}") for m in range(3)]
        (o_sel, o_gath, o_xg, o_gate, o_up, o_gread, o_sig, o_hid, o_hidT_mm, o_hidT, o_wselT_mm, o_wselT,
         o_down, o_yg, o_scat) = (sem(f"o_{n}") for n in (
             "sel", "gath", "xg", "gate", "up", "gread", "sig", "hid", "hidT_mm", "hidT", "wselT_mm", "wselT",
             "down", "yg", "scat"))
        N_LIST = EXTRA * E

        def more_passes(eng, body):
            eng.wait_ge(meta_ready, 1)
            count = eng.value_load(meta[0:1, 2 * N_LIST:2 * N_LIST + 1], min_val=0, max_val=N_LIST)
            with eng.If(count > 0):
                with eng.Fori(0, count) as m:
                    body(m)
            return count

        def expert_of(eng, m):
            return eng.value_load(meta[0:1, bass.ds(m, 1)], min_val=0, max_val=E - 1)

        def place_of(eng, m):
            return eng.value_load(meta[0:1, bass.ds(m + N_LIST, 1)], min_val=CAP, max_val=CAP * EXTRA)

        block = ctx.enter_context(nc.Block())

        @block.sync
        def _(sp):
            half = KT // 2
            xT_d = a["xT"].rearrange("(k p) t -> p k t", p=P)

            def load(kind, e, s, h):
                src = a[kind][bass.ds(e, 1)].rearrange("o (k p) n -> p (o k) n", p=P)
                k = slice(h * half, (h + 1) * half)
                sp.dma_start(slot[:, s, k], src[:, k]).then_inc(d_slot[s][h], 16)

            sp.dma_start(cols[:], a["cols"]).then_inc(d_cols, 16)
            for h in range(2):
                k = slice(h * half, (h + 1) * half)
                sp.dma_start(xT[:, k], xT_d[:, k]).then_inc(d_xT[h], 16)
                sp.dma_start(w_conv[:, 0, k], a["w_conv"][0][:, k]).then_inc(d_conv[CC * h], 16)
            for c in range(1, CC):
                sp.dma_start(w_conv[:, c], a["w_conv"][c]).then_inc(d_conv[c], 16)
            sp.dma_start(w_qk, a["w_qk"].rearrange("c p k n -> p c k n")).then_inc(d_qk, 16)
            sp.dma_start(w_v, a["w_v"]).then_inc(d_v, 16)
            sp.dma_start(relb, a["relb"]).then_inc(d_rel, 16)
            for h in range(2):
                load("w_gate", 0, 0, h)
            for h in range(2):
                load("w_up", 0, 1, h)
            sp.wait_ge(conv_mm, CC)
            sp.dma_start(w_out, a["w_out"].rearrange("(k p) n -> p k n", p=P)).then_inc(d_wout, 16)
            sp.dma_start(router_w[:], a["router_w"].rearrange("(k p) e -> p k e", p=P)).then_inc(d_small, 16)
            sp.dma_start(router_b[:], a["router_b"]).then_inc(d_small, 16)
            sp.dma_start(bias_gu[:], a["bias_gu"]).then_inc(d_bias, 16)
            sp.wait_ge(qk_mm, 4)
            for h in range(2):
                load("w_gate", 1, 3, h)
            sp.wait_ge(v_mm, TT)
            load("w_down", 0, 2, 0)
            sp.wait_ge(conv_ready, CC)
            sp.dma_start(gain_ffn, a["gain_ffn"]).then_inc(d_gffn, 16)
            sp.wait_ge(score_read, HEADS)
            load("w_down", 0, 2, 1)
            sp.wait_ge(probsT_mm, HEADS)
            sp.dma_start(late[:], a["gain_last"]).then_inc(d_gfin, 16)
            sp.wait_ge(out_mm, 2 * TT)
            for h in range(2):
                load("w_up", 1, 4, h)
            sp.wait_ge(cleared, 1)
            sp.dma_start(yg[0:E, 0], a["b_down"][:, 0:HB]).then_inc(d_yg, 16)
            sp.dma_start(yg[CAP:CAP + E, 1], a["b_down"][:, HB:D]).then_inc(d_yg, 16)

            with sp.Fori(0, PAIRS - 1) as i:
                for j in range(2):
                    n = i * 2 + j
                    for h in range(2):
                        sp.wait_ge(gate_mm, n * 2 + h + 1)
                        load("w_gate", n + 2, GATE[j], h)
                    for h in range(2):
                        sp.wait_ge(up_mm, n * 2 + h + 1)
                        load("w_up", n + 2, UP[j], h)
                    for h in range(2):
                        sp.wait_ge(down_mm, n * 2 + h + 1)
                        load("w_down", n + 1, 2, h)
            for q in range(4):
                k = slice(q * 2, q * 2 + 2)
                sp.wait_ge(down_mm, 2 * E - 3 + q // 2)
                sp.dma_start(slot[:, 2, k], a["w_down"][E - 1].rearrange("(k p) n -> p k n", p=P)[:, k]).then_inc(
                    d_last[q], 16)

            def weights_again(m):
                e = expert_of(sp, m)
                sp.wait_ge(down_mm, 2 * E)
                sp.wait_ge(o_scat, m + 1)
                for k, kind in enumerate(("w_gate", "w_up", "w_down")):
                    src = a[kind][bass.ds(e, 1)].rearrange("o (k p) n -> p (o k) n", p=P)
                    sp.dma_start(slot[:, k], src).then_inc(o_slot[k], 16)

            more_passes(sp, weights_again)
            for t in range(TT):
                for h in range(2):
                    sp.wait_ge(fin_ready, 2 * t + h + 1)
                    sp.dma_start(out.rearrange("(t p) d -> p t d", p=P)[:, t, h * HB:(h + 1) * HB],
                                 outb[:, t, h * HB:(h + 1) * HB]).then_inc(d_out, 16)
            sp.wait_ge(d_out, 16 * 2 * TT)

        @block.gpsimd
        def _(pool):
            g = nc.gpsimd
            st = Steps(pool, pool_step)

            def one(ins):
                st.mark(ins)
                st.wait()

            one(g.memset(ones[:], 1.0))
            one(g.memset(ident_w[:], 0.0))
            g.affine_select(out=ident, in_=ident, compare_op=ALU.not_equal, fill=1.0, base=0,
                            pattern=[[-1, P]], channel_multiplier=1).then_inc(ident_ready, 1)
            pool.wait_ge(ident_ready, 1)
            one(g.memset(padded[:, :, 0:PAD], 0.0))
            one(g.memset(before[:], 1.0))
            one(g.affine_select(out=before[:], in_=before[:], compare_op=ALU.is_gt, fill=0.0, base=0,
                                pattern=[[1, P]], channel_multiplier=-1))
            one(g.iota(iota[:], pattern=[[1, T]], base=0, channel_multiplier=0, allow_small_or_imprecise_dtypes=True))
            for c in range(EXTRA):
                q = slice(32 * c, 32 * c + 32)
                one(g.iota(code_e[q], pattern=[[0, 1]], base=0, channel_multiplier=1,
                           allow_small_or_imprecise_dtypes=True))
                one(g.memset(code_c[q], float(CAP * (c + 1))))
                one(g.memset(thresh[q], float(CAP * (c + 1))))
            one(g.memset(rank[:], -1.0))
            one(g.memset(share[:], 0.0))
            g.memset(dummy, 1.0).then_inc(const_ready, 1)
            pool.wait_ge(const_ready, 1)
            pool.wait_ge(h2_ready, 2 * TT)
            g.memset(yg, 0.0).then_inc(cleared, 1)

        @block.scalar
        def _(act):
            s = nc.scalar
            def table(func, n):
                s.activation(dummy[:, 1:2], dummy[:, 0:1], func).then_inc(act_step, 1)
                act.wait_ge(act_step, n)

            for h in range(2):
                act.wait_ge(d_xT[h], 16)
                s.activation(xsq[:, 4 * h:4 * h + 4], xT[:, 4 * h:4 * h + 4], ACT.Square).then_inc(sq_ready, 1)
            act.wait_ge(var_ready, 1)
            s.activation(rstd_row, rstd_row, ACT.Sqrt).then_inc(sd_ready, 1)
            for c in range(CC):
                act.wait_ge(gate_in, c + 1)
                s.activation(sgate[:, c], sgate[:, c], ACT.Sigmoid).then_inc(sgate_ready, 1)
            act.wait_ge(col_ready, 1)
            for t in range(TT):
                act.wait_ge(v_mm, t + 1)
                s.activation(val[:, t], bank[t][:], ACT.Copy, scale=rstd_col[:, t:t + 1]).then_inc(v_ready, 1)
            act.wait_ge(const_ready, 1)
            table(ACT.Sqrt, 1)
            act.wait_ge(cent_ready, 1)
            s.activation(lnsq, acc, ACT.Square).then_inc(lnsq_ready, 1)
            act.wait_ge(lnv_ready, 1)
            s.activation(lnrow[:, 0], lnrow[:, 0], ACT.Sqrt).then_inc(lnsd_ready, 1)
            table(ACT.Sigmoid, 2)
            for c in range(CC):
                act.wait_ge(xn_ready, c + 1)
                s.activation(padded[:, c, 0:T], acc[:, c], ACT.Sigmoid, bias=ln_b[:, c:c + 1],
                             scale=ln_g[:, c:c + 1]).then_inc(lnsig_ready, 1)
            table(ACT.Exp, 3)

            def exps(h):
                p, q = h % 2, 2 * (h % 2)
                act.wait_ge(max_ready, h + 1)
                s.activation(probs[:, p, 0:T], probs[:, p, 0:T], ACT.Exp, bias=negmax[:, q:q + 1],
                             accum_out=den[:, q:q + 1])
                s.activation(probs[:, p, T:3 * P], probs[:, p, T:3 * P], ACT.Exp, bias=negmax[:, q + 1:q + 2],
                             accum_out=den[:, q + 1:q + 2]).then_inc(exp_ready, 1)

            exps(0)
            for h in range(HEADS):
                if h + 1 < HEADS:
                    exps(h + 1)
                act.wait_ge(probsT_mm, h + 1)
                s.activation(probsT[:, h % 2], b6[:, 0:3 * P], ACT.Copy).then_inc(probsT_ready, 1)
                if h % 2 == 1:
                    c = h // 2
                    act.wait_ge(av_mm, c + 1)
                    s.activation(mixT[:, c], b7[:, (c % 2) * T:(c % 2 + 1) * T], ACT.Copy).then_inc(av_ready, 1)
            table(ACT.Sqrt, 4)
            for t in range(TT):
                for h in range(2):
                    n = 2 * t + h
                    act.wait_ge(out_mm, n + 1)
                    s.activation(hT_flat[:, n * HB:(n + 1) * HB], y[:, n], ACT.Square,
                                 accum_out=ssq[:, n:n + 1]).then_inc(ssq_ready, 1)
                act.wait_ge(ms_ready, t + 1)
                s.activation(rstd[:, t:t + 1], rstd[:, t:t + 1], ACT.Sqrt).then_inc(rms_sd, 1)
            table(ACT.Exp, 5)
            for t in range(TT):
                act.wait_ge(h2T_mm, 2 * t + 1)
                s.activation(hT[:, 0:4, t * P:(t + 1) * P], bank[2 * t][:].rearrange("p (k n) -> p k n", k=4),
                             ACT.Copy).then_inc(h2T_act, 1)
            act.wait_ge(top_shift, 1)
            s.activation(topw, topw, ACT.Exp).then_inc(top_exp, 1)
            table(ACT.Sigmoid, 6)
            act.wait_ge(wselT_mm, 1)
            s.activation(wselT.rearrange("p o t -> p (o t)"), b5[:], ACT.Copy).then_inc(wselT_ready, 1)

            with act.Fori(0, PAIRS) as i:
                for j in range(2):
                    n = i * 2 + j
                    act.wait_ge(gate_ready, n + 1)
                    s.activation(sig, gate, ACT.Sigmoid, scale=ALPHA).then_inc(sig_ready, 1)
                    act.wait_ge(hidT_mm, n + 1)
                    s.activation(hidT.rearrange("p a b -> p (a b)"), b5[:], ACT.Copy).then_inc(hidT_ready, 1)
                act.wait_ge(down_mm, i * 4 + 4)
                s.activation(yg[:, 0], b6[:], ACT.Copy)
                s.activation(yg[:, 1], b7[:], ACT.Copy).then_inc(yg_ready, 1)
                act.wait_ge(wselT_mm, i + 2)
                s.activation(wselT.rearrange("p o t -> p (o t)"), b5[:], ACT.Copy).then_inc(wselT_ready, 1)

            def again(m):
                act.wait_ge(o_wselT_mm, m + 1)
                s.activation(wselT.rearrange("p o t -> p (o t)"), b7[:], ACT.Copy).then_inc(o_wselT, 1)
                act.wait_ge(o_gread, m + 1)
                s.activation(sig, gate, ACT.Sigmoid, scale=ALPHA).then_inc(o_sig, 1)
                act.wait_ge(o_hidT_mm, m + 1)
                s.activation(hidT.rearrange("p a b -> p (a b)"), b5[:], ACT.Copy).then_inc(o_hidT, 1)
                act.wait_ge(o_down, m + 1)
                s.activation(yg[0:CAP, 0], b6[0:CAP], ACT.Copy)
                s.activation(yg[CAP:P, 1], b7[CAP:P], ACT.Copy).then_inc(o_yg, 1)

            count = more_passes(act, again)
            table(ACT.Sqrt, 7)
            act.wait_ge(o_scat, count + 1)
            for t in range(TT):
                s.activation(slot[:, 1, t], y[:, 2 * t:2 * t + 2].rearrange("p h n -> p (h n)"), ACT.Square,
                             accum_out=fsq[:, t:t + 1]).then_inc(fsq_ready, 1)
            for t in range(TT):
                act.wait_ge(fms_ready, t + 1)
                s.activation(frstd[:, t:t + 1], frstd[:, t:t + 1], ACT.Sqrt).then_inc(fsd_ready, 1)

        @block.vector
        def _(dve):
            v = nc.vector
            st = Steps(dve, dve_step)
            dve.wait_ge(d_cols, 16)
            for k in range(KT):
                if k % 4 == 0:
                    dve.wait_ge(d_xT[k // 4], 16)
                v.tensor_scalar(hT[:, k], xT[:, k], g_mix[:, k:k + 1], None, ALU.mult).then_inc(hT_ready, 1)
            dve.wait_ge(ssum_done, 1)
            v.tensor_scalar(rstd_row, b7[:, 0:T], 1.0 / D, EPS, ALU.mult, ALU.add).then_inc(var_ready, 1)
            dve.wait_ge(sd_ready, 1)
            v.reciprocal(rstd_row, rstd_row).then_inc(norm_ready, 1)
            dve.wait_ge(norm_ready, 1)
            dve.wait_ge(col_mm, 1)
            v.tensor_copy(rstd_col, b6[:, 0:2]).then_inc(col_ready, 1)
            dve.wait_ge(const_ready, 1)
            dve.wait_ge(seed_mm, 1)
            last = [0] * CC

            def conv_in(c):
                dve.wait_ge(conv_mm, c + 1)
                v.tensor_tensor(sgate[:, c], bank[c][:, T:2 * T], rstd_row, ALU.mult).then_inc(gate_in, 1)
                n = st.mark(v.tensor_tensor(padded[:, c, PAD:PAD + T], bank[c][:, 0:T], rstd_row, ALU.mult))
                st.wait(n)
                dve.wait_ge(sgate_ready, c + 1)
                v.tensor_tensor(padded[:, c, PAD:PAD + T], padded[:, c, PAD:PAD + T], sgate[:, c],
                                ALU.mult).then_inc(conv_read, 1)

            def tap(c, k):
                if k == 0:
                    ins = v.tensor_scalar(acc[:, c], padded[:, c, 0:T], dw[:, c, 0:1], dw_b[:, c:c + 1],
                                          ALU.mult, ALU.add)
                else:
                    st.wait(last[c])
                    ins = v.scalar_tensor_tensor(out=acc[:, c], in0=padded[:, c, k:k + T], scalar=dw[:, c, k:k + 1],
                                                 in1=acc[:, c], op0=ALU.mult, op1=ALU.add)
                if k < TAPS - 1:
                    last[c] = st.mark(ins)
                else:
                    ins.then_inc(acc_ready, 1)

            def qk_out(c):
                dve.wait_ge(qk_mm, c + 1)
                v.tensor_tensor(qkT[:, c], bank[c][:].rearrange("p (w t) -> p w t", w=2),
                                rstd_row.unsqueeze(1).to_broadcast([P, 2, T]), ALU.mult).then_inc(qk_ready, 1)

            conv_in(0)
            conv_in(1)
            dve.wait_ge(conv_read, 2)
            for k in range(TAPS):
                for c in (0, 1):
                    tap(c, k)
                if k in (TAPS // 3, 2 * TAPS // 3):
                    conv_in(2 if k == TAPS // 3 else 3)
            dve.wait_ge(conv_read, CC)
            for k in range(TAPS):
                for c in (2, 3):
                    tap(c, k)
                if k in (2, 12, 22):
                    qk_out(k // 10)
            qk_out(3)
            dve.wait_ge(acc_ready, CC)
            dve.wait_ge(mu_mm, 1)
            for c in range(CC):
                ins = v.scalar_tensor_tensor(out=acc[:, c], in0=b6[:, 0:T], scalar=-1.0 / D_CONV, in1=acc[:, c],
                                             op0=ALU.mult, op1=ALU.add)
            ins.then_inc(cent_ready, 1)
            dve.wait_ge(d_rel, 16)
            st.mark(v.memset(relb[0:64, :, T - 64:T], MASKED))
            st.wait()

            def softmax_in(h):
                p, q = h % 2, 2 * (h % 2)
                dve.wait_ge(score_mm, h + 1)
                if h >= 2:
                    dve.wait_ge(probsT_mm, h - 1)
                v.scalar_tensor_tensor(out=probs[:, p, 0:T], in0=bank[p][:, 0:T], scalar=HD ** -0.5,
                                       in1=relb[:, h], op0=ALU.mult, op1=ALU.add)
                v.scalar_tensor_tensor(out=probs[:, p, T:3 * P], in0=bank[p][:, T:3 * P], scalar=HD ** -0.5,
                                       in1=relb[:, h, P:T], op0=ALU.mult, op1=ALU.add).then_inc(score_read, 1)
                dve.wait_ge(score_read, h + 1)
                v.tensor_reduce(negmax[:, q:q + 1], probs[:, p, 0:T], AX.X, ALU.max, negate=True)
                v.tensor_reduce(negmax[:, q + 1:q + 2], probs[:, p, T:3 * P], AX.X, ALU.max,
                                negate=True).then_inc(max_ready, 1)

            def softmax_out(h):
                p, q = h % 2, 2 * (h % 2)
                dve.wait_ge(exp_ready, h + 1)
                st.mark(v.reciprocal(rden[:, q:q + 2], den[:, q:q + 2]))
                st.wait()
                v.tensor_scalar(probs[:, p, 0:T], probs[:, p, 0:T], rden[:, q:q + 1], None, ALU.mult)
                v.tensor_scalar(probs[:, p, T:3 * P], probs[:, p, T:3 * P], rden[:, q + 1:q + 2], None,
                                ALU.mult).then_inc(probs_ready, 1)

            softmax_in(0)
            softmax_in(1)
            dve.wait_ge(lnv_mm, 1)
            v.tensor_scalar(lnrow[:, 0], b7[:, 0:T], 1.0 / D_CONV, EPS, ALU.mult, ALU.add).then_inc(lnv_ready, 1)
            dve.wait_ge(lnsd_ready, 1)
            st.mark(v.reciprocal(lnrow[:, 0], lnrow[:, 0]))
            st.wait()
            for c in range(CC):
                v.tensor_tensor(acc[:, c], acc[:, c], lnrow[:, 0], ALU.mult).then_inc(xn_ready, 1)
            for c in range(CC):
                dve.wait_ge(lnsig_ready, c + 1)
                last[c] = st.mark(v.tensor_scalar(acc[:, c], acc[:, c], ln_g[:, c:c + 1], ln_b[:, c:c + 1],
                                                  ALU.mult, ALU.add))
            for c in range(CC):
                st.wait(last[c])
                v.tensor_tensor(mixT[:, CC + c], acc[:, c], padded[:, c, 0:T], ALU.mult).then_inc(conv_ready, 1)
            for h in range(HEADS):
                softmax_out(h)
                if h + 2 < HEADS:
                    softmax_in(h + 2)
            dve.wait_ge(d_gffn, 16)
            for t in range(TT):
                dve.wait_ge(ssq_ready, 2 * t + 2)
                st.mark(v.tensor_tensor(rstd[:, t:t + 1], ssq[:, 2 * t:2 * t + 1], ssq[:, 2 * t + 1:2 * t + 2], ALU.add))
                st.wait()
                v.tensor_scalar(rstd[:, t:t + 1], rstd[:, t:t + 1], 1.0 / D, EPS, ALU.mult,
                                ALU.add).then_inc(ms_ready, 1)
                dve.wait_ge(rms_sd, t + 1)
                st.mark(v.reciprocal(rstd[:, t:t + 1], rstd[:, t:t + 1]))
                st.wait()
                for h in range(2):
                    v.scalar_tensor_tensor(out=h2[:, t, h * HB:(h + 1) * HB], in0=y[:, 2 * t + h],
                                           scalar=rstd[:, t:t + 1], in1=gain_ffn[:, h * HB:(h + 1) * HB],
                                           op0=ALU.mult, op1=ALU.mult).then_inc(h2_ready, 1)
                if t == 0:
                    continue
                for tt in range(TT):
                    dve.wait_ge(h2T_mm, 2 * tt + 2)
                    v.tensor_copy(hT[:, 4:8, tt * P:(tt + 1) * P],
                                  bank[2 * tt + 1][:].rearrange("p (k n) -> p k n", k=4)).then_inc(h2T_dve, 1)
            dve.wait_ge(lg_mm, 1)
            v.tensor_copy(lgT, b4[:, 0:T]).then_inc(lgT_ready, 1)
            dve.wait_ge(lgt_mm, 1)
            st.mark(v.tensor_reduce(lg, b5[:, 0:T].rearrange("p (t q e) -> p t e q", t=TT, q=4), AX.X, ALU.add))
            st.wait()
            dve.wait_ge(d_small, 32)
            st.mark(v.tensor_tensor(lg, lg, router_b[:].unsqueeze(1).to_broadcast([P, TT, E]), ALU.add))
            st.wait()
            for t in range(TT):
                ins = v.max(topv[:, t], lg[:, t])
            st.mark(ins)
            st.wait()
            for t in range(TT):
                v.max_index(topi[:, t], topv[:, t], lg[:, t])
            v.tensor_tensor(topw, topv[:, :, 0:TOPK], topv[:, :, 0:1].to_broadcast([P, TT, TOPK]),
                            ALU.subtract).then_inc(top_shift, 1)
            dve.wait_ge(top_shift, 1)
            st.mark(v.tensor_copy(topf, topi[:, :, 0:TOPK]))
            st.wait()
            st.mark(v.tensor_tensor(hit.rearrange("p (t k) e -> p t k e", t=TT),
                                    iota[:, 0:E].unsqueeze(1).unsqueeze(1).to_broadcast([P, TT, TOPK, E]),
                                    topf.unsqueeze(3).to_broadcast([P, TT, TOPK, E]), ALU.is_equal))
            st.wait()
            v.tensor_reduce(mask, hit.rearrange("p (t k) e -> p t e k", t=TT), AX.X, ALU.add).then_inc(mask_ready, 1)
            dve.wait_ge(mask_ready, 1)
            v.tensor_copy(mask3.rearrange("p t (c e) -> p t c e", c=EXTRA),
                          mask.unsqueeze(2).to_broadcast([P, TT, EXTRA, E])).then_inc(mask_ready, 1)
            dve.wait_ge(top_exp, 1)
            st.mark(v.tensor_reduce(wsum, topw, AX.X, ALU.add))
            st.wait()
            st.mark(v.reciprocal(wsum, wsum))
            st.wait()
            st.mark(v.tensor_tensor(topw, topw, wsum.unsqueeze(2).to_broadcast([P, TT, TOPK]), ALU.mult))
            st.wait()
            st.mark(v.tensor_tensor(whit.rearrange("p (t k) e -> p t k e", t=TT),
                                    hit.rearrange("p (t k) e -> p t k e", t=TT),
                                    topw.unsqueeze(3).to_broadcast([P, TT, TOPK, E]), ALU.mult))
            st.wait()
            st.mark(v.tensor_reduce(share[:, :, 0:E], whit.rearrange("p (t k) e -> p t e k", t=TT), AX.X, ALU.add))
            dve.wait_ge(rank_mm, 1)
            st.mark(v.scalar_tensor_tensor(out=rank[:, :, 0:E], in0=b6[:, 0:TT * E].rearrange("p (t e) -> p t e", t=TT),
                                           scalar=1.0, in1=mask, op0=ALU.add, op1=ALU.mult))
            st.wait()
            st.mark(v.tensor_scalar(rank[:, :, 0:E], rank[:, :, 0:E], -1.0, None, ALU.add))
            st.wait()

            def build_sel(e, places, width):
                k = width // CAP
                return v.tensor_tensor(
                    sel[:, :, 0:width].rearrange("p t (k c) -> p t k c", k=k),
                    places.unsqueeze(1).unsqueeze(1).to_broadcast([P, TT, k, CAP]),
                    rank[:, :, bass.ds(e, k)].unsqueeze(3).to_broadcast([P, TT, k, CAP]), ALU.is_equal)

            def build_wsel(e, k):
                v.tensor_tensor(wsel[:, :, 0:k * CAP].rearrange("p t (k c) -> p t k c", k=k),
                                sel[:, :, 0:k * CAP].rearrange("p t (k c) -> p t k c", k=k),
                                share[:, :, bass.ds(e, k)].unsqueeze(3).to_broadcast([P, TT, k, CAP]), ALU.mult)
                return v.tensor_tensor(wsel[:, :, 2 * CAP:3 * CAP], sel[:, :, 0:CAP],
                                       share[:, :, bass.ds(e, 1)].to_broadcast([P, TT, CAP]), ALU.mult)

            def build_pick(e, j):
                src = ident_w[:, bass.ds(e, 4, E)]
                return v.tensor_copy(pick[:, j], src.unsqueeze(2).to_broadcast([P, 4, CAP]))

            build_sel(0, iota[:, 0:CAP], 2 * CAP).then_inc(sel_ready, 1)
            st.mark(v.memset(wsel, 0.0))
            st.wait()
            v.tensor_copy(wsel[:, :, 0:E], share[:, :, 0:E])
            v.tensor_copy(wsel[:, :, 2 * CAP:2 * CAP + E], share[:, :, 0:E]).then_inc(wsel_ready, 1)
            for j in range(2):
                ins = build_pick(j, j)
            ins.then_inc(pick_ready, 1)
            for k in range(2):
                dve.wait_ge(gath_mm, k + 1)
                v.tensor_copy(xg[:, 4 * k:4 * k + 4].rearrange("p a b -> p (a b)"),
                              bank[2 * k][:]).then_inc(xg_ready, 1)
            dve.wait_ge(cnt_mm, 1)
            v.tensor_scalar(flag[0:N_LIST], b7[0:N_LIST, 0:1], thresh[0:N_LIST], None, ALU.is_gt).then_inc(flag_ready, 1)
            dve.wait_ge(place_mm, 1)
            v.tensor_scalar(onehot[0:N_LIST], iota[0:N_LIST, 0:N_LIST], b7[0:N_LIST, 1:2], flag[0:N_LIST],
                            ALU.is_equal, ALU.mult).then_inc(onehot_ready, 1)
            dve.wait_ge(list_mm, 1)
            v.tensor_copy(meta[0:1, 0:2 * N_LIST + 1], b7[0:1, 8:8 + 2 * N_LIST + 1]).then_inc(meta_ready, 1)

            with dve.Fori(0, PAIRS) as i:
                dve.wait_ge(wselT_mm, i + 1)
                dve.wait_ge(sel_ready, i + 1)
                build_wsel(i * 2, 2).then_inc(wsel_ready, 1)
                for j in range(2):
                    n = i * 2 + j
                    dve.wait_ge(gate_mm, n * 2 + 2)
                    v.tensor_scalar(gate, b4[:], LIMIT, None, ALU.min).then_inc(gate_ready, 1)
                    if j == 0:
                        dve.wait_ge(wsel_ready, i + 2)
                        build_sel(i * 2 + 2, iota[:, 0:CAP], 2 * CAP).then_inc(sel_ready, 1)
                    dve.wait_ge(sig_ready, n + 1)
                    v.tensor_tensor(sig, gate, sig, ALU.mult).then_inc(part_ready, 1)
                    dve.wait_ge(up_mm, n * 2 + 2)
                    v.tensor_scalar(up, b5[:], LIMIT, -LIMIT, ALU.min, ALU.max).then_inc(up_ready, 1)
                    dve.wait_ge(part_ready, n + 1)
                    dve.wait_ge(up_ready, n + 1)
                    v.scalar_tensor_tensor(out=hid, in0=up, scalar=1.0, in1=sig, op0=ALU.add,
                                           op1=ALU.mult).then_inc(hid_ready, 1)
                for k in range(2):
                    dve.wait_ge(gath_mm, i * 2 + 3 + k)
                    v.tensor_copy(xg[:, 4 * k:4 * k + 4].rearrange("p a b -> p (a b)"), b4[:]).then_inc(xg_ready, 1)
                for j in range(2):
                    ins = build_pick(i * 2 + 2 + j, j)
                ins.then_inc(pick_ready, 1)

            def again(m):
                e = expert_of(dve, m)
                first = place_of(dve, m)
                dve.wait_ge(o_scat, m + 1)
                dve.wait_ge(pick_ready, PAIRS + 1)
                build_sel(e, iota[:, bass.ds(first, CAP)], CAP).then_inc(dve_over, 1)
                build_pick(e, 0)
                dve.wait_ge(dve_over, m + 1)
                build_wsel(e, 1).then_inc(o_sel, 1)
                dve.wait_ge(o_gath, m + 1)
                v.tensor_copy(xg[:, :, 0:CAP], b4[:].rearrange("p (k c) -> p k c", k=KT)).then_inc(o_xg, 1)
                dve.wait_ge(o_gate, m + 1)
                v.tensor_scalar(gate, b4[:], LIMIT, None, ALU.min).then_inc(o_gread, 1)
                dve.wait_ge(o_up, m + 1)
                v.tensor_scalar(up, b5[:], LIMIT, -LIMIT, ALU.min, ALU.max)
                dve.wait_ge(o_sig, m + 1)
                v.tensor_tensor(sig, gate, sig, ALU.mult).then_inc(dve_tail, 1)
                dve.wait_ge(dve_tail, m + 1)
                v.scalar_tensor_tensor(out=hid, in0=up, scalar=1.0, in1=sig, op0=ALU.add,
                                       op1=ALU.mult).then_inc(o_hid, 1)

            count = more_passes(dve, again)
            dve.wait_ge(o_scat, count + 1)
            dve.wait_ge(d_gfin, 16)
            for t in range(TT):
                dve.wait_ge(fsq_ready, t + 1)
                v.tensor_scalar(frstd[:, t:t + 1], fsq[:, t:t + 1], 1.0 / D, EPS, ALU.mult,
                                ALU.add).then_inc(fms_ready, 1)
            for t in range(TT):
                dve.wait_ge(fsd_ready, t + 1)
                st.mark(v.reciprocal(frstd[:, t:t + 1], frstd[:, t:t + 1]))
                st.wait()
                for h in range(2):
                    v.scalar_tensor_tensor(out=outb[:, t, h * HB:(h + 1) * HB], in0=y[:, 2 * t + h],
                                           scalar=frstd[:, t:t + 1], in1=late[:, h * HB:(h + 1) * HB],
                                           op0=ALU.mult, op1=ALU.mult).then_inc(fin_ready, 1)

        @block.tensor
        def _(pe):
            def mm(o, l, r, start, stop=False, **kw):
                return pe.matmul(o, l, r, start=start, stop=stop, skip_group_check=True, **kw)

            pe.wait_ge(ident_ready, 1)
            for h in range(2):
                pe.wait_ge(d_xT[h], 16)
                for k in range(4 * h, 4 * h + 4):
                    for t in range(TT):
                        last = pe.matmul(y[:, 2 * t + h, (k % 4) * P:(k % 4 + 1) * P], xT[:, k, t * P:(t + 1) * P],
                                         ident, start=k % 4 == 0, stop=k % 4 == 3, is_transpose=True,
                                         skip_group_check=True)
                if h == 1:
                    last.then_inc(seed_mm, 1)
                pe.wait_ge(sq_ready, h + 1)
                for k in range(4 * h, 4 * h + 4):
                    last = mm(b7[:, 0:T], ones[:], xsq[:, k], k == 0, k == KT - 1)
            last.then_inc(ssum_done, 1)
            for c in range(CC):
                if c == 1:
                    pe.wait_ge(norm_ready, 1)
                    for t in range(TT):
                        last = mm(b6[:, t:t + 1], rstd_row[0:1, t * P:(t + 1) * P], ones[0:1, 0:1], True, True)
                    last.then_inc(col_mm, 1)
                if c == 2:
                    pe.wait_ge(col_ready, 1)
                if c == 3:
                    pe.wait_ge(var_ready, 1)
                pe.wait_ge(d_conv[c], 16)
                for w in range(2):
                    for k in range(KT):
                        if c == 0 and w == 0:
                            if k == 4:
                                pe.wait_ge(d_conv[CC], 16)
                            pe.wait_ge(hT_ready, k + 1)
                        last = mm(bank[c][:, w * T:(w + 1) * T], w_conv[:, c, k, w * P:(w + 1) * P], hT[:, k],
                                  k == 0, k == KT - 1)
                last.then_inc(conv_mm, 1)
            pe.wait_ge(d_qk, 16)
            for c in range(4):
                pe.wait_ge(conv_read, c + 1)
                for w in range(2):
                    for k in range(KT):
                        last = mm(bank[c][:, w * T:(w + 1) * T], w_qk[:, c, k, w * P:(w + 1) * P], hT[:, k],
                                  k == 0, k == KT - 1)
                last.then_inc(qk_mm, 1)
            pe.wait_ge(d_v, 16)
            for t in range(TT):
                pe.wait_ge(qk_ready, t + 1)
                for k in range(KT):
                    last = mm(bank[t][:], hT[:, k, t * P:(t + 1) * P], w_v[:, k], k == 0, k == KT - 1)
                last.then_inc(v_mm, 1)

            def scores(h):
                c, lo, b = h // 2, (h % 2) * HD, bank[h % 2]
                r = slice(lo, lo + HD)
                if h < 2:
                    pe.wait_ge(v_ready, h + 1)
                else:
                    pe.wait_ge(score_read, h - 1)
                mm(b[:, 0:T], qkT[r, c, 0, P:T], qkT[r, c, 1, 0:T], True, True)
                mm(b[:, T:3 * P], qkT[r, c, 0, 0:P], qkT[r, c, 1, 0:P], True, True).then_inc(score_mm, 1)

            scores(0)
            scores(1)
            pe.wait_ge(acc_ready, CC)
            pe.wait_ge(qk_ready, 4)
            for c in range(CC):
                last = mm(b6[:, 0:T], ones[:], acc[:, c], c == 0, c == CC - 1)
            last.then_inc(mu_mm, 1)
            pe.wait_ge(lnsq_ready, 1)
            for c in range(CC):
                last = mm(b7[:, 0:T], ones[:], lnsq[:, c], c == 0, c == CC - 1)
            last.then_inc(lnv_mm, 1)

            def out_part(k, t, h):
                return mm(y[:, 2 * t + h], mixT[:, k, t * P:(t + 1) * P], w_out[:, k, h * HB:(h + 1) * HB], False,
                          k == 3)

            def probs_T(h):
                pe.wait_ge(probs_ready, h + 1)
                if h >= 1:
                    pe.wait_ge(probsT_ready, h)
                for o, i in ((0, T), (P, 0), (T, P)):
                    last = pe.transpose(b6[:, o:o + P], probs[:, h % 2, i:i + P], ident)
                last.then_inc(probsT_mm, 1)
                if h + 2 < HEADS:
                    scores(h + 2)

            early = [(k, t, h) for k in range(4, 8) for t in range(TT) for h in range(2)]
            pe.wait_ge(cent_ready, 1)
            pe.wait_ge(lnv_ready, 1)
            for c in range(HEADS // 2):
                for h in (2 * c, 2 * c + 1):
                    probs_T(h)
                    if c == 0 and h == 0:
                        pe.wait_ge(conv_ready, CC)
                        pe.wait_ge(d_wout, 16)
                    for e in early[2 * h:2 * h + 2]:
                        out_part(*e)
                pe.wait_ge(probsT_ready, 2 * c + 2)
                if c >= 2:
                    pe.wait_ge(av_ready, c - 1)
                at = (c % 2) * T
                for k in range(TT):
                    for p in range(2):
                        r, hd = slice(p * HD, p * HD + HD), (2 * c + p) * HD
                        last = mm(b7[r, at + k * P:at + T], val[:, k, hd:hd + HD],
                                  probsT[:, p, k * T:T + k * P], k == 0, k == 1)
                last.then_inc(av_mm, 1)
            for t in range(TT):
                for h in range(2):
                    for k in range(4):
                        if t == 0 and h == 0:
                            pe.wait_ge(av_ready, k + 1)
                        last = out_part(k, t, h)
                    last.then_inc(out_mm, 1)

            for t in range(TT):
                for k in range(KT):
                    if k % 4 == 0:
                        pe.wait_ge(h2_ready, 2 * t + k // 4 + 1)
                    last = pe.transpose(bank[2 * t + k // 4][:, (k % 4) * P:(k % 4 + 1) * P],
                                        h2[:, t, k * P:(k + 1) * P], ident)
                    if k % 4 == 3:
                        last.then_inc(h2T_mm, 1)
            pe.wait_ge(h2T_act, TT)
            pe.wait_ge(h2T_dve, TT)
            pe.wait_ge(d_small, 32)
            for r in range(2):
                for q in range(4):
                    k = 4 * r + q
                    last = mm(b4[32 * q:32 * q + 32, 0:T], router_w[:, k], hT[:, k], r == 0, r == 1)
            last.then_inc(lg_mm, 1)
            pe.wait_ge(lgT_ready, 1)
            for t in range(TT):
                last = pe.transpose(b5[:, t * P:(t + 1) * P], lgT[:, t * P:(t + 1) * P], ident)
            last.then_inc(lgt_mm, 1)
            pe.wait_ge(mask_ready, 1)
            mm(b6[:, 0:E], before[:], mask[:, 0], True, True)
            mm(b6[:, E:2 * E], ones[:], mask[:, 0], True)
            mm(b6[:, E:2 * E], before[:], mask[:, 1], False, True).then_inc(rank_mm, 1)

            def gather(k, o, width):
                n = HB // width
                for kk in range(n):
                    for t in range(TT):
                        f = (k + kk) * P
                        last = mm(o[:, kk * width:(kk + 1) * width], h2[:, t, f:f + P], sel[:, t, 0:width],
                                  t == 0, t == TT - 1)
                return last

            def weigh_T(o):
                for order in range(2):
                    for t in range(TT):
                        at = (order * TT + t) * P
                        last = pe.transpose(o[:, at:at + P], wsel[:, t, order * CAP:order * CAP + P], ident)
                return last

            def k_tiles(w, waits, count, halves, product):
                for k in range(KT):
                    for wait in waits.get(k, ()):
                        pe.wait_ge(*wait)
                    last = product(k, w[:, k])
                    if k == KT - 1 or (halves and k == KT // 2 - 1):
                        last.then_inc(count, 1)

            def project(o, lhs, w, waits, bias, j, count, halves=True):
                for h in range(2):
                    mm(o[h * CAP:(h + 1) * CAP, :], pick[:, j, bias + h], bias_gu[:], True)

                def product(k, wk):
                    for h in range(2):
                        last = mm(o[h * CAP:(h + 1) * CAP, :], lhs(k), wk[:, h * HB:(h + 1) * HB], False, k == KT - 1)
                    return last

                k_tiles(w, waits, count, halves, product)

            def down(outs, w, waits, j, count, halves=True):
                def product(k, wk):
                    for h in range(2):
                        q = h ^ j
                        last = mm(outs[h][q * CAP:(q + 1) * CAP, :],
                                  hidT[:, k % 4, (k // 4) * CAP:(k // 4 + 1) * CAP],
                                  wk[:, h * HB:(h + 1) * HB], k == 0, k == KT - 1)
                    return last

                k_tiles(w, waits, count, halves, product)

            def hid_T(o):
                for c in range(4):
                    last = pe.transpose(o[:, c * P:(c + 1) * P], hid[:, c * P:(c + 1) * P], ident)
                return last

            def scatter(h, ts, rows=slice(0, P)):
                for t in ts:
                    last = mm(y[:, 2 * t + h], wselT[rows, h, t * P:(t + 1) * P], yg[rows, h], False)
                return last

            pe.wait_ge(sel_ready, 1)
            gather(0, b4, 2 * CAP).then_inc(gath_mm, 1)
            gather(4, b6, 2 * CAP).then_inc(gath_mm, 1)
            pe.wait_ge(wsel_ready, 1)
            weigh_T(b5).then_inc(wselT_mm, 1)
            pe.wait_ge(mask_ready, 2)
            for t in range(TT):
                last = mm(b7[0:N_LIST, 0:1], mask3[:, t], ones[:, 0:1], t == 0, t == TT - 1)
            last.then_inc(cnt_mm, 1)
            pe.wait_ge(flag_ready, 1)
            mm(b7[0:N_LIST, 1:2], before[0:N_LIST, 0:N_LIST], flag[0:N_LIST], True, True).then_inc(place_mm, 1)
            pe.wait_ge(onehot_ready, 1)
            mm(b7[0:1, 8:8 + N_LIST], code_e[0:N_LIST], onehot[0:N_LIST], True, True)
            mm(b7[0:1, 8 + N_LIST:8 + 2 * N_LIST], code_c[0:N_LIST], onehot[0:N_LIST], True, True)
            mm(b7[0:1, 8 + 2 * N_LIST:9 + 2 * N_LIST], flag[0:N_LIST], ones[0:N_LIST, 0:1], True,
               True).then_inc(list_mm, 1)
            pe.wait_ge(d_bias, 16)
            pe.wait_ge(d_yg, 32)
            pe.wait_ge(meta_ready, 1)

            def pair(i, last_down=None):
                for j in range(2):
                    n = i * 2 + j

                    def loaded(sl, count):
                        return {h * KT // 2: [(d_slot[sl][h], count * 16)] for h in range(2)}

                    def tokens(k):
                        return xg[:, k, j * CAP:(j + 1) * CAP]

                    waits = loaded(GATE[j], i + 1)
                    if j == 0:
                        pe.wait_ge(pick_ready, i + 1)
                        pe.wait_ge(xg_ready, i * 2 + 1)
                        waits[KT // 2].append((xg_ready, i * 2 + 2))
                    project(b4, tokens, slot[:, GATE[j]], waits, 0, j, gate_mm)
                    if j == 0:
                        pe.wait_ge(wselT_ready, i + 1)
                    project(b5, tokens, slot[:, UP[j]], loaded(UP[j], i + 1), 2, j, up_mm)
                    if j == 0:
                        scatter(0, range(TT))
                        pe.wait_ge(hid_ready, n + 1)
                        hid_T(b5).then_inc(hidT_mm, 1)
                        scatter(1, range(TT)).then_inc(scat_mm, 1)
                    else:
                        pe.wait_ge(sel_ready, i + 2)
                        pe.wait_ge(gate_ready, n + 1)
                        gather(0, b4, 2 * CAP).then_inc(gath_mm, 1)
                        pe.wait_ge(hid_ready, n + 1)
                        hid_T(b5).then_inc(hidT_mm, 1)
                        pe.wait_ge(xg_ready, i * 2 + 3)
                        gather(4, b4, 2 * CAP).then_inc(gath_mm, 1)
                    pe.wait_ge(hidT_ready, n + 1)
                    if j == 1 and last_down:
                        pe.wait_ge(wsel_ready, i + 2)
                        weigh_T(b5).then_inc(wselT_mm, 1)
                        down((b6, b7), slot[:, 2], last_down, j, down_mm)
                    else:
                        down((b6, b7), slot[:, 2], loaded(2, n + 1), j, down_mm)
                        if j == 1:
                            pe.wait_ge(wsel_ready, i + 2)
                            weigh_T(b5).then_inc(wselT_mm, 1)

            with pe.Fori(0, PAIRS - 1) as i:
                pair(i)
            pair(PAIRS - 1, {2 * q: [(d_last[q], 16)] for q in range(4)})
            pe.wait_ge(wselT_ready, PAIRS + 1)
            pe.wait_ge(yg_ready, PAIRS)
            scatter(0, range(TT)).then_inc(scat_mm, 1)
            scatter(1, range(TT)).then_inc(o_scat, 1)

            def again(m):
                pe.wait_ge(o_sel, m + 1)
                gather(0, b4, CAP).then_inc(o_gath, 1)
                weigh_T(b7).then_inc(o_wselT_mm, 1)
                pe.wait_ge(o_xg, m + 1)
                lhs = lambda k: xg[:, k, 0:CAP]
                loaded = lambda k: {0: [(o_slot[k], (m + 1) * 16)]}
                project(b4, lhs, slot[:, 0], loaded(0), 0, 0, o_gate, halves=False)
                project(b5, lhs, slot[:, 1], loaded(1), 2, 0, o_up, halves=False)
                pe.wait_ge(o_hid, m + 1)
                hid_T(b5).then_inc(o_hidT_mm, 1)
                pe.wait_ge(o_hidT, m + 1)
                pe.wait_ge(o_wselT, m + 1)
                down((b6, b7), slot[:, 2], loaded(2), 0, o_down, halves=False)
                pe.wait_ge(o_yg, m + 1)
                scatter(0, range(TT), slice(0, CAP))
                scatter(1, range(TT), slice(CAP, P)).then_inc(o_scat, 1)

            more_passes(pe, again)


_SHAPES = ["xT", "cols", "w_conv", "w_qk", "w_v", "relb", "w_out", "gain_ffn", "router_w", "router_b", "bias_gu",
           "w_gate", "w_up", "w_down", "b_down", "gain_last"]


def _lay_out(x, norm_mix_g, w_in, conv_dw_w, conv_dw_b, conv_ln_g, conv_ln_b, rel_bias, w_out, norm_ffn_g, router_w,
             router_b, exp_w_gate, exp_b_gate, exp_w_up, exp_b_up, exp_w_down, exp_b_down, norm_final_g):
    import numpy as np

    def columns(v):
        return v.reshape(-1, P).T

    def rows(v):
        return np.ascontiguousarray(np.broadcast_to(v, (P, v.shape[-1])))

    w = w_in[0].reshape(KT, P, -1).transpose(1, 0, 2)
    q, k, v, conv, gate = (w[:, :, i * HB:(i + 1) * HB] for i in range(5))

    def pairs(l, r):
        return np.ascontiguousarray(np.stack(
            [np.concatenate([l[:, :, c * P:(c + 1) * P], r[:, :, c * P:(c + 1) * P]], axis=2) for c in range(4)]))

    back = rel_bias[0][:, ::-1]
    ext = np.concatenate([np.repeat(back[:, :1], P - 1, axis=1), back, np.repeat(back[:, -1:], 64, axis=1)], axis=1)
    relb = np.stack([ext[:, P - 1 - p:P - 1 - p + T] for p in range(P)])
    taps = conv_dw_w[0].T.reshape(CC, P, TAPS).transpose(1, 0, 2).reshape(P, CC * TAPS)
    bg, bu = exp_b_gate[0], exp_b_up[0]
    return {
        "xT": x[0].T,
        "cols": np.concatenate([columns(norm_mix_g[0]), taps, columns(conv_dw_b[0]), columns(conv_ln_g[0]),
                                columns(conv_ln_b[0])], axis=1),
        "w_conv": pairs(conv, gate), "w_qk": pairs(q, k), "w_v": v, "relb": relb, "w_out": w_out[0],
        "gain_ffn": rows(norm_ffn_g[0]), "router_w": router_w[0], "router_b": rows(router_b[0]),
        "bias_gu": np.concatenate([bg[:, :HB], bg[:, HB:], bu[:, :HB], bu[:, HB:]], axis=0),
        "w_gate": exp_w_gate[0], "w_up": exp_w_up[0], "w_down": exp_w_down[0], "b_down": exp_b_down[0],
        "gain_last": rows(norm_final_g),
    }


def kernel(**inputs):
    import numpy as np
    import concourse.bacc as bacc
    from concourse.bass_utils import run_bass_kernel_spmd

    laid = _lay_out(**{k: np.asarray(v) for k, v in inputs.items()})
    nc = bacc.Bacc("TRN2", target_bir_lowering=False, num_devices=1)
    arrays, args = {}, {}
    for name in _SHAPES:
        v = np.ascontiguousarray(laid[name])
        arrays[f"in_{name}"] = v
        args[name] = nc.dram_tensor(f"in_{name}", v.shape, mybir.dt.from_np(v.dtype), kind="ExternalInput").ap()
    out = nc.dram_tensor("out_y", (T, D), F32, kind="ExternalOutput").ap()
    build_block(nc, args, out)
    r = run_bass_kernel_spmd(nc, [arrays], core_ids=[0])
    return r.results[0]["out_y"].reshape(1, T, D)
```

```python
from contextlib import ExitStack

import concourse.bass as bass
from concourse import mybir

P = 128
F32 = mybir.dt.float32
I32 = mybir.dt.int32
U32 = mybir.dt.uint32
ALU = mybir.AluOpType
ACT = mybir.ActivationFunctionType
AX = mybir.AxisListType

D = 1024
T = 256
KT = D // P
TT = T // P
HEADS, HD = 8, 64
D_ATTN = HEADS * HD
D_CONV = 512
CC = D_CONV // P
TAPS = 31
PAD = TAPS - 1
E = 32
TOPK = 4
CAP = 64
EXTRA = T // CAP - 1
PAIRS = E // 2
LIMIT = 7.0
ALPHA = 1.702
PIECES = 4
PK = KT // PIECES
WARM_UP = 8
HEAD_START = 10
EPS = 1e-5
MASKED = -1e30
HB = 512


class Steps:

    def __init__(self, eng, sem):
        self.eng, self.sem, self.n = eng, sem, 0

    def mark(self, ins):
        ins.then_inc(self.sem, 1)
        self.n += 1
        return self.n

    def wait(self, n=None):
        self.eng.wait_ge(self.sem, self.n if n is None else n)


def build_block(nc, a, out):
    with ExitStack() as ctx:
        def sb(name, shape, dt=F32):
            return ctx.enter_context(nc.sbuf_tensor(name, shape, dt))

        def psum(name, shape):
            return ctx.enter_context(nc.psum_tensor(name, shape, F32))

        def sem(name):
            return ctx.enter_context(nc.semaphore(name))

        y = psum("y", [P, 2 * TT, HB])
        b4, b5, b6, b7 = (psum(f"b{i}", [P, HB]) for i in range(4, 8))
        bank = [b4, b5, b6, b7]
        hb = [b5, b6]

        slot = sb("slot", [P, 5, KT, D])
        GATE, UP, DOWN = (0, 3), (1, 4), 2
        work = sb("work", [P, 6392])
        h2 = sb("h2", [P, TT, D])
        late = sb("late", [P, D])
        probsT = sb("probsT", [P, 2, 3 * P])
        router_w = sb("router_w", [P, KT, E])
        router_b = sb("router_b", [P, E])
        ident_w = sb("ident_w", [P, P])
        ident = ident_w[:]
        ones = sb("ones", [P, P])
        before = sb("before", [P, P])
        iota = sb("iota", [P, T + 1])
        bias_gu = sb("bias_gu", [P, HB])
        rank = sb("rank", [P, TT, E])
        share = sb("share", [P, TT, E])
        cols = sb("cols", [P, KT + CC * TAPS + 3 * CC])
        sm = sb("sm", [P, 64])
        meta = sb("meta", [1, 2 * EXTRA * E + 8], I32)

        def part(t, at, shape):
            n = 1
            for s in shape:
                n *= s
            v = t[:, at:at + n]
            if len(shape) == 1:
                return v
            names = "abc"[:len(shape)]
            return v.rearrange(f"p ({' '.join(names)}) -> p {' '.join(names)}",
                               **{c: s for c, s in zip(names[1:], shape[1:])})

        xg = part(work, 0, [KT, 2 * CAP])
        hid = part(work, 1024, [HB])
        hidT = part(work, 1536, [4, P])
        gate = part(work, 2048, [HB])
        up = part(work, 2560, [HB])
        yg = part(work, 3072, [2, HB])
        sel = part(work, 4216, [TT, 2 * CAP])
        wsel = part(work, 4472, [TT, 3 * CAP])
        wselT = part(work, 4856, [2, T])
        pick = part(work, 5368, [2, 4, CAP])
        sig = part(work, 5880, [HB])
        hT = part(work, 0, [KT, T])
        rstd_row = part(late, 768, [T])
        val = part(work, 2048, [TT, D_ATTN])
        gain_ffn = part(work, 3072, [D])
        padded = part(work, 3072, [CC, PAD + T])
        lnsq = part(work, 3072, [CC, T])
        mixT = part(work, 4216, [2 * CC, T])
        xsq = part(work, 4216, [KT, T])
        h2f = h2[:].rearrange("p t d -> p (t d)")
        xT = part(h2f, 0, [KT, T])
        acc = part(h2f, 0, [CC, T])
        junk = [h2[:, 1, 0:HB], h2[:, 1, HB:D], probsT[:].rearrange("p h k -> p (h k)")[:, 0:HB],
                part(work, 4216, [HB])]
        sgate = part(h2f, 1024, [CC, T])
        lnrow = part(h2f, 1024, [CC, T])
        probs = part(late, 0, [2, 3 * P])
        sumsq = part(late, 0, [T])
        lgT = part(work, 2048, [T])
        lg = part(work, 2304, [TT, E])
        hit = part(work, 2368, [TT * TOPK, E])
        whit = part(work, 2624, [TT * TOPK, E])
        mask = part(work, 2880, [TT, E])
        mask3 = part(work, 2048, [TT, EXTRA * E])
        xtok = part(work, 1024, [D])
        w_conv = slot[:, 4].rearrange("p a b -> p (a b)").rearrange("p (c k n) -> p c k n", c=CC, k=KT)
        w_qk = slot[:, 3].rearrange("p a b -> p (a b)").rearrange("p (c k n) -> p c k n", c=4, k=KT)
        w_out = slot[:, 4]
        s2 = slot[:, 2].rearrange("p a b -> p (a b)")
        w_v = s2[:, 0:4096].rearrange("p (k n) -> p k n", k=KT)
        qkT = s2[:, 4096:6144].rearrange("p (c w t) -> p c w t", c=4, w=2)
        relb = s2[:, 6144:8192].rearrange("p (h k) -> p h k", h=HEADS)
        wselT_more = part(slot[:, 3, 0], 0, [2, T])
        yg_more = part(slot[:, 3, 1], 0, [2, HB])
        outb = slot[:, 0].rearrange("p a b -> p (a b)")[:, 0:TT * D].rearrange("p (t d) -> p t d", t=TT)
        g_mix = cols[:, 0:KT]
        dw = cols[:, KT:KT + CC * TAPS].rearrange("p (c k) -> p c k", c=CC)
        c0 = KT + CC * TAPS
        dw_b, ln_g, ln_b = (cols[:, c0 + i * CC:c0 + (i + 1) * CC] for i in range(3))
        negmax, den, rden = sm[:, 0:4], sm[:, 4:8], sm[:, 8:12]
        ssq, rstd = sm[:, 16:20], sm[:, 14:16]
        fsq, frstd = sm[:, 0:4], sm[:, 4:6]
        topv = sm[:, 20:36].rearrange("p (t k) -> p t k", t=TT)
        topw = sm[:, 36:44].rearrange("p (t k) -> p t k", t=TT)
        topi = sb("topi", [P, TT, 8], U32)
        topf = sm[:, 44:52].rearrange("p (t k) -> p t k", t=TT)
        wsum = sm[:, 52:54]
        rstd_col = sm[:, 59:61]
        dummy = sm[0:1, 61:63]
        code_e, code_c, thresh, flag = (sm[:, 54 + i:55 + i] for i in range(4))
        onehot = part(work, 2048 + TT * EXTRA * E, [EXTRA * E])

        d_cols, d_qk, d_v, d_wout, d_rel, d_small, d_gffn, d_bias, d_yg, d_gfin, d_out = (
            sem(f"d_{n}") for n in ("cols", "qk", "v", "wout", "rel", "small", "gffn",
                                    "bias", "yg", "gfin", "out"))
        d_xT = [sem(f"d_xT{h}") for h in range(2)]
        d_conv = [sem(f"d_conv{c}") for c in range(CC + 1)]
        d_last = [sem(f"d_last{k}") for k in range(PK)]
        d_slot = [[sem(f"d_slot{s}{q}") for q in range(PIECES)] for s in range(5)]
        (ident_ready, const_ready, cleared, relb_ready, pool_step, dve_step, act_step, dve_tail, dve_over) = (
            sem(n) for n in ("ident_ready", "const_ready", "cleared", "relb_ready", "pool_step", "dve_step",
                "act_step", "dve_tail", "dve_over"))
        (sq_ready, sumsq_ready, ssum_done, var_ready, sd_ready, norm_ready, col_mm, col_ready, seed_mm,
         hT_ready, conv_mm, gate_in, sgate_ready, conv_read, qk_mm, qk_ready, v_mm, v_ready) = (
            sem(n) for n in ("sq_ready", "sumsq_ready", "ssum_done", "var_ready", "sd_ready", "norm_ready",
                "col_mm", "col_ready", "seed_mm", "hT_ready", "conv_mm", "gate_in", "sgate_ready",
                "conv_read", "qk_mm", "qk_ready", "v_mm", "v_ready"))
        (acc_ready, mu_mm, cent_ready, lnsq_ready, lnv_mm, lnv_ready, lnsd_ready, xn_ready, lnsig_ready,
         conv_ready) = (
            sem(n) for n in ("acc_ready", "mu_mm", "cent_ready", "lnsq_ready", "lnv_mm", "lnv_ready",
                "lnsd_ready", "xn_ready", "lnsig_ready", "conv_ready"))
        (score_mm, score_read, max_ready, exp_ready, rden_ready, probs_ready, probsT_mm, probsT_ready, av_mm,
         av_ready) = (
            sem(n) for n in ("score_mm", "score_read", "max_ready", "exp_ready", "rden_ready",
                "probs_ready", "probsT_mm", "probsT_ready", "av_mm", "av_ready"))
        (out_mm, gained, ssq_ready, ms_ready, rms_sd, rms_ready, h2_ready, h2T_mm, h2T_act, h2T_dve, lg_mm,
         lgT_ready, lgt_mm, lgt_read, top_shift, top_exp, mask_ready, rank_mm) = (
            sem(n) for n in ("out_mm", "gained", "ssq_ready", "ms_ready", "rms_sd", "rms_ready", "h2_ready",
                "h2T_mm", "h2T_act", "h2T_dve", "lg_mm", "lgT_ready", "lgt_mm", "lgt_read", "top_shift",
                "top_exp", "mask_ready", "rank_mm"))
        (cnt_mm, flag_ready, place_mm, onehot_ready, list_mm, meta_ready, xtok_dve, xtok_act, xtokT_mm) = (
            sem(n) for n in ("cnt_mm", "flag_ready", "place_mm", "onehot_ready", "list_mm", "meta_ready",
                "xtok_dve", "xtok_act", "xtokT_mm"))
        (sel_ready, gath_mm, xg_ready, pick_ready, gate_mm, gate_ready, sig_ready, part_ready, up_mm,
         up_ready, hid_ready, hidT_mm, hidT_ready, down_mm, half_mm, yg_ready, yg_last, wsel_ready,
         wselT_mm, wselT_ready) = (
            sem(n) for n in ("sel_ready", "gath_mm", "xg_ready", "pick_ready", "gate_mm", "gate_ready",
                "sig_ready", "part_ready", "up_mm", "up_ready", "hid_ready", "hidT_mm", "hidT_ready",
                "down_mm", "half_mm", "yg_ready", "yg_last", "wsel_ready", "wselT_mm", "wselT_ready"))
        (fin_mm, fsq_ready, fms_ready, fsd_ready, fin_ready) = (
            sem(n) for n in ("fin_mm", "fsq_ready", "fms_ready", "fsd_ready", "fin_ready"))
        o_slot = [sem(f"o_slot{m}") for m in range(3)]
        (o_sel, o_gath, o_xg, o_gate, o_up, o_gread, o_sig, o_hid, o_hidT_mm, o_hidT, o_wselT_mm, o_wselT,
         o_down, o_yg, o_scat) = (sem(f"o_{n}") for n in (
             "sel", "gath", "xg", "gate", "up", "gread", "sig", "hid", "hidT_mm", "hidT", "wselT_mm", "wselT",
             "down", "yg", "scat"))
        N_LIST = EXTRA * E

        def more_passes(eng, body):
            eng.wait_ge(meta_ready, 1)
            count = eng.value_load(meta[0:1, 2 * N_LIST:2 * N_LIST + 1], min_val=0, max_val=N_LIST)
            with eng.If(count > 0):
                with eng.Fori(0, count) as m:
                    body(m)
            return count

        def expert_of(eng, m):
            return eng.value_load(meta[0:1, bass.ds(m, 1)], min_val=0, max_val=E - 1)

        def place_of(eng, m):
            return eng.value_load(meta[0:1, bass.ds(m + N_LIST, 1)], min_val=CAP, max_val=CAP * EXTRA)

        block = ctx.enter_context(nc.Block())

        @block.sync
        def _(sp):
            xT_d = a["xT"].rearrange("(k p) t -> p k t", p=P)

            def load(kind, e, s, pieces=range(PIECES), wait=None):
                src = a[kind][bass.ds(e, 1)].rearrange("o (k p) n -> p (o k) n", p=P)
                for q in pieces:
                    if wait:
                        sp.wait_ge(wait[0], wait[1] + q)
                    k = slice(q * PK, (q + 1) * PK)
                    sp.dma_start(slot[:, s, k], src[:, k]).then_inc(d_slot[s][q], 16)

            sp.dma_start(cols[:], a["cols"]).then_inc(d_cols, 16)
            for h in range(2):
                k = slice(h * KT // 2, (h + 1) * KT // 2)
                sp.dma_start(xT[:, k], xT_d[:, k]).then_inc(d_xT[h], 16)
                sp.dma_start(w_conv[:, 0, k], a["w_conv"][0][:, k]).then_inc(d_conv[CC * h], 16)
            for c in range(1, CC):
                sp.dma_start(w_conv[:, c], a["w_conv"][c]).then_inc(d_conv[c], 16)
            sp.dma_start(w_v, a["w_v"]).then_inc(d_v, 16)
            sp.dma_start(w_qk, a["w_qk"].rearrange("c p k n -> p c k n")).then_inc(d_qk, 16)
            sp.dma_start(relb, a["relb"]).then_inc(d_rel, 16)
            load("w_gate", 0, 0)
            load("w_up", 0, 1)
            sp.wait_ge(conv_mm, CC)
            sp.dma_start(w_out, a["w_out"].rearrange("(k p) n -> p k n", p=P)).then_inc(d_wout, 16)
            sp.dma_start(router_w[:], a["router_w"].rearrange("(k p) e -> p k e", p=P)).then_inc(d_small, 16)
            sp.dma_start(router_b[:], a["router_b"]).then_inc(d_small, 16)
            sp.dma_start(bias_gu[:], a["bias_gu"]).then_inc(d_bias, 16)
            sp.wait_ge(v_mm, TT)
            load("w_down", 0, 2, range(PIECES // 2))
            sp.wait_ge(qk_mm, 4)
            load("w_gate", 1, 3)
            sp.wait_ge(score_read, HEADS)
            load("w_down", 0, 2, range(PIECES // 2, PIECES))
            sp.wait_ge(probsT_mm, HEADS)
            sp.dma_start(late[:], a["gain_last"]).then_inc(d_gfin, 16)
            sp.wait_ge(conv_ready, CC)
            sp.dma_start(gain_ffn, a["gain_ffn"]).then_inc(d_gffn, 16)
            sp.wait_ge(out_mm, 2 * TT)
            load("w_up", 1, 4)
            sp.wait_ge(cleared, 1)
            sp.dma_start(yg[0:E, 0], a["b_down"][:, 0:HB]).then_inc(d_yg, 16)
            sp.dma_start(yg[CAP:CAP + E, 1], a["b_down"][:, HB:D]).then_inc(d_yg, 16)

            def next_gate(n, j):
                load("w_gate", n + 2, GATE[j], wait=(gate_mm, n * PIECES + 1))

            def next_up(n, j):
                load("w_up", n + 2, UP[j], wait=(up_mm, n * PIECES + 1))

            def next_down(n):
                load("w_down", n + 1, DOWN, wait=(down_mm, n * PIECES + 1))

            with sp.Fori(0, PAIRS - 2) as i:
                for j in range(2):
                    n = i * 2 + j
                    next_gate(n, j)
                    next_up(n, j)
                    next_down(n)
            for j in range(2):
                n = E - 4 + j
                next_gate(n, j)
                if j == 0:
                    next_down(n)
                    next_up(n, j)
                else:
                    next_up(n, j)
                    next_down(n)
            load("w_down", E - 1, GATE[0], range(PIECES - 1), (gate_mm, (E - 2) * PIECES + 1))
            sp.wait_ge(gate_mm, (E - 1) * PIECES)
            for k in range(PK):
                at = KT - PK + k
                src = a["w_down"][E - 1].rearrange("(k p) n -> p k n", p=P)
                sp.dma_start(slot[:, GATE[0], at], src[:, at]).then_inc(d_last[k], 16)

            def weights_again(m):
                e = expert_of(sp, m)
                sp.wait_ge(down_mm, PIECES * E)
                sp.wait_ge(o_scat, m + 1)
                for k, kind in enumerate(("w_gate", "w_up", "w_down")):
                    src = a[kind][bass.ds(e, 1)].rearrange("o (k p) n -> p (o k) n", p=P)
                    sp.dma_start(slot[:, k], src).then_inc(o_slot[k], 16)

            more_passes(sp, weights_again)
            for t in range(TT):
                for h in range(2):
                    sp.wait_ge(fin_ready, 2 * t + h + 1)
                    sp.dma_start(out.rearrange("(t p) d -> p t d", p=P)[:, t, h * HB:(h + 1) * HB],
                                 outb[:, t, h * HB:(h + 1) * HB]).then_inc(d_out, 16)
            sp.wait_ge(d_out, 16 * 2 * TT)

        @block.gpsimd
        def _(pool):
            g = nc.gpsimd
            st = Steps(pool, pool_step)

            def one(ins):
                st.mark(ins)
                st.wait()

            one(g.memset(ones[:], 1.0))
            one(g.memset(ident_w[:], 0.0))
            g.affine_select(out=ident, in_=ident, compare_op=ALU.not_equal, fill=1.0, base=0,
                            pattern=[[-1, P]], channel_multiplier=1).then_inc(ident_ready, 1)
            pool.wait_ge(ident_ready, 1)
            one(g.memset(padded[:, :, 0:PAD], 0.0))
            one(g.memset(before[:], 1.0))
            one(g.affine_select(out=before[:], in_=before[:], compare_op=ALU.is_gt, fill=0.0, base=0,
                                pattern=[[1, P]], channel_multiplier=-1))
            one(g.iota(iota[:], pattern=[[1, T + 1]], base=0, channel_multiplier=0,
                       allow_small_or_imprecise_dtypes=True))
            for c in range(EXTRA):
                q = slice(32 * c, 32 * c + 32)
                one(g.iota(code_e[q], pattern=[[0, 1]], base=0, channel_multiplier=1,
                           allow_small_or_imprecise_dtypes=True))
                one(g.memset(code_c[q], float(CAP * (c + 1))))
                one(g.memset(thresh[q], float(CAP * (c + 1))))
            g.memset(dummy, 1.0).then_inc(const_ready, 1)
            pool.wait_ge(d_rel, 16)
            g.memset(relb[0:64, :, T - 64:T], MASKED).then_inc(relb_ready, 1)
            pool.wait_ge(const_ready, 1)
            pool.wait_ge(gained, 2 * TT)
            g.memset(yg, 0.0).then_inc(cleared, 1)

        @block.scalar
        def _(act):
            s = nc.scalar
            def table(func, n):
                s.activation(dummy[:, 1:2], dummy[:, 0:1], func).then_inc(act_step, 1)
                act.wait_ge(act_step, n)

            for h in range(2):
                act.wait_ge(d_xT[h], 16)
                s.activation(xsq[:, 4 * h:4 * h + 4], xT[:, 4 * h:4 * h + 4], ACT.Square).then_inc(sq_ready, 1)
            act.wait_ge(var_ready, 1)
            s.activation(rstd_row, rstd_row, ACT.Sqrt).then_inc(sd_ready, 1)
            for c in range(CC):
                act.wait_ge(gate_in, c + 1)
                s.activation(sgate[:, c], sgate[:, c], ACT.Sigmoid).then_inc(sgate_ready, 1)
            act.wait_ge(col_ready, 1)
            for t in range(TT):
                act.wait_ge(v_mm, t + 1)
                s.activation(val[:, t], bank[t][:], ACT.Copy, scale=rstd_col[:, t:t + 1]).then_inc(v_ready, 1)
            act.wait_ge(const_ready, 1)
            table(ACT.Exp, 1)

            def exps(h):
                p, q = h % 2, 2 * (h % 2)
                act.wait_ge(max_ready, h + 1)
                s.activation(probs[:, p, 0:T], probs[:, p, 0:T], ACT.Exp, bias=negmax[:, q:q + 1],
                             accum_out=den[:, q:q + 1])
                s.activation(probs[:, p, T:3 * P], probs[:, p, T:3 * P], ACT.Exp, bias=negmax[:, q + 1:q + 2],
                             accum_out=den[:, q + 1:q + 2]).then_inc(exp_ready, 1)

            def normalise(h):
                p, q = h % 2, 2 * (h % 2)
                act.wait_ge(exp_ready, h + 1)
                act.wait_ge(rden_ready, h + 1)
                s.activation(probs[:, p, 0:T], probs[:, p, 0:T], ACT.Copy, scale=rden[:, q:q + 1])
                s.activation(probs[:, p, T:3 * P], probs[:, p, T:3 * P], ACT.Copy,
                             scale=rden[:, q + 1:q + 2]).then_inc(probs_ready, 1)

            def probs_T_out(c):
                for h in (2 * c, 2 * c + 1):
                    act.wait_ge(probsT_mm, h + 1)
                    s.activation(probsT[:, h % 2], hb[h % 2][:, 0:3 * P], ACT.Copy).then_inc(probsT_ready, 1)

            def values_out(c):
                act.wait_ge(av_mm, c + 1)
                s.activation(mixT[:, c], b7[:, (c % 2) * T:(c % 2 + 1) * T], ACT.Copy).then_inc(av_ready, 1)

            for c in range(HEADS // 2):
                pair_of_heads = (2 * c, 2 * c + 1)
                for h in pair_of_heads:
                    exps(h)
                for h in pair_of_heads:
                    normalise(h)
                probs_T_out(c)
                if c < HEADS // 2 - 1:
                    values_out(c)
            table(ACT.Sqrt, 2)
            for c in range(CC):
                act.wait_ge(cent_ready, c + 1)
                s.activation(lnsq[:, c], acc[:, c], ACT.Square).then_inc(lnsq_ready, 1)
            act.wait_ge(lnv_ready, 1)
            s.activation(lnrow[:, 0], lnrow[:, 0], ACT.Sqrt).then_inc(lnsd_ready, 1)
            table(ACT.Sigmoid, 3)
            values_out(HEADS // 2 - 1)
            for c in range(CC):
                act.wait_ge(xn_ready, c + 1)
                s.activation(padded[:, c, 0:T], acc[:, c], ACT.Sigmoid, bias=ln_b[:, c:c + 1],
                             scale=ln_g[:, c:c + 1]).then_inc(lnsig_ready, 1)
            table(ACT.Sqrt, 4)
            def square(t, h):
                n = 2 * t + h
                act.wait_ge(gained, n + 1)
                s.activation(junk[n], y[:, n], ACT.Square, accum_out=ssq[:, n:n + 1]).then_inc(ssq_ready, 1)

            def h2T_out(t):
                act.wait_ge(h2T_mm, 2 * t + 1)
                s.activation(hT[:, 0:4, t * P:(t + 1) * P], b4[:].rearrange("p (k n) -> p k n", k=4),
                             ACT.Copy).then_inc(h2T_act, 1)

            def second_rms(t):
                act.wait_ge(ssq_ready, 2 * t + 2)
                act.wait_ge(ms_ready, t + 1)
                s.activation(rstd[:, t:t + 1], ssq[:, 2 * t + 1:2 * t + 2], ACT.Sqrt, bias=rstd[:, t:t + 1],
                             scale=1.0 / D).then_inc(rms_sd, 1)

            def scale_h2(t):
                act.wait_ge(rms_ready, t + 1)
                act.wait_ge(h2T_mm, 2 * t + 2)
                s.activation(h2[:, t], h2[:, t], ACT.Copy, scale=rstd[:, t:t + 1]).then_inc(h2_ready, 1)

            square(0, 0)
            square(0, 1)
            second_rms(0)
            h2T_out(0)
            scale_h2(0)
            square(1, 0)
            h2T_out(1)
            square(1, 1)
            second_rms(1)
            scale_h2(1)
            table(ACT.Exp, 5)
            act.wait_ge(top_shift, TT)
            s.activation(topw, topw, ACT.Exp).then_inc(top_exp, 1)
            table(ACT.Sigmoid, 6)
            act.wait_ge(gath_mm, 2)
            s.activation(xtok[:, HB:D], b6[:], ACT.Copy).then_inc(xtok_act, 1)
            act.wait_ge(wselT_mm, 1)
            s.activation(wselT.rearrange("p o t -> p (o t)"), b5[:], ACT.Copy).then_inc(wselT_ready, 1)

            def gate_and_hidden(n):
                act.wait_ge(gate_ready, n + 1)
                s.activation(sig, gate, ACT.Sigmoid, scale=ALPHA).then_inc(sig_ready, 1)
                act.wait_ge(hidT_mm, n + 1)
                s.activation(hidT.rearrange("p a b -> p (a b)"), b5[:], ACT.Copy).then_inc(hidT_ready, 1)

            def weights_T(n, src):
                act.wait_ge(wselT_mm, n)
                s.activation(wselT.rearrange("p o t -> p (o t)"), src, ACT.Copy).then_inc(wselT_ready, 1)

            with act.Fori(0, PAIRS - 1) as i:
                for j in range(2):
                    gate_and_hidden(i * 2 + j)
                act.wait_ge(down_mm, (i + 1) * (2 * PIECES))
                s.activation(yg[:, 0], b6[:], ACT.Copy)
                s.activation(yg[:, 1], b7[:], ACT.Copy).then_inc(yg_ready, 1)
                weights_T(i + 2, b5[:])
            gate_and_hidden(E - 2)
            weights_T(PAIRS + 1, b6[:])
            gate_and_hidden(E - 1)
            act.wait_ge(half_mm, 1)
            s.activation(yg[:, 0], b6[:], ACT.Copy).then_inc(yg_ready, 1)

            def again(m):
                act.wait_ge(o_wselT_mm, m + 1)
                s.activation(wselT_more.rearrange("p o t -> p (o t)"), b7[:], ACT.Copy).then_inc(o_wselT, 1)
                act.wait_ge(o_gread, m + 1)
                s.activation(sig, gate, ACT.Sigmoid, scale=ALPHA).then_inc(o_sig, 1)
                act.wait_ge(o_hidT_mm, m + 1)
                s.activation(hidT.rearrange("p a b -> p (a b)"), b5[:], ACT.Copy).then_inc(o_hidT, 1)
                act.wait_ge(o_down, m + 1)
                s.activation(yg_more[0:CAP, 0], b6[0:CAP], ACT.Copy)
                s.activation(yg_more[CAP:P, 1], b7[CAP:P], ACT.Copy).then_inc(o_yg, 1)

            more_passes(act, again)
            table(ACT.Sqrt, 7)
            for t in range(TT):
                for h in range(2):
                    n = 2 * t + h
                    act.wait_ge(fin_mm, n + 1)
                    s.activation(slot[:, UP[0], n, 0:HB], y[:, n], ACT.Square,
                                 accum_out=fsq[:, n:n + 1]).then_inc(fsq_ready, 1)
                act.wait_ge(fsq_ready, 2 * t + 2)
                act.wait_ge(fms_ready, t + 1)
                s.activation(frstd[:, t:t + 1], fsq[:, 2 * t + 1:2 * t + 2], ACT.Sqrt, bias=frstd[:, t:t + 1],
                             scale=1.0 / D).then_inc(fsd_ready, 1)

        @block.vector
        def _(dve):
            v = nc.vector
            st = Steps(dve, dve_step)
            dve.wait_ge(d_cols, 16)
            for k in range(KT):
                if k % 4 == 0:
                    dve.wait_ge(d_xT[k // 4], 16)
                v.tensor_scalar(hT[:, k], xT[:, k], g_mix[:, k:k + 1], None, ALU.mult).then_inc(hT_ready, 1)
            dve.wait_ge(sq_ready, 2)
            v.tensor_reduce(sumsq, xsq.rearrange("p k t -> p t k"), AX.X, ALU.add).then_inc(sumsq_ready, 1)
            dve.wait_ge(ssum_done, 1)
            v.tensor_scalar(rstd_row, b7[:, 0:T], 1.0 / D, EPS, ALU.mult, ALU.add).then_inc(var_ready, 1)
            dve.wait_ge(sd_ready, 1)
            v.reciprocal(rstd_row, rstd_row).then_inc(norm_ready, 1)
            dve.wait_ge(norm_ready, 1)
            dve.wait_ge(const_ready, 1)
            dve.wait_ge(seed_mm, 1)
            last = [0] * CC

            def conv_in(c):
                dve.wait_ge(conv_mm, c + 1)
                v.tensor_tensor(sgate[:, c], bank[c][:, T:2 * T], rstd_row, ALU.mult).then_inc(gate_in, 1)
                n = st.mark(v.tensor_tensor(padded[:, c, PAD:PAD + T], bank[c][:, 0:T], rstd_row, ALU.mult))
                st.wait(n)

            def conv_gate(c):
                dve.wait_ge(sgate_ready, c + 1)
                v.tensor_tensor(padded[:, c, PAD:PAD + T], padded[:, c, PAD:PAD + T], sgate[:, c],
                                ALU.mult).then_inc(conv_read, 1)

            def tap(c, k):
                if k == 0:
                    dve.wait_ge(conv_read, c + 1)
                    ins = v.tensor_scalar(acc[:, c], padded[:, c, 0:T], dw[:, c, 0:1], dw_b[:, c:c + 1],
                                          ALU.mult, ALU.add)
                else:
                    st.wait(last[c])
                    ins = v.scalar_tensor_tensor(out=acc[:, c], in0=padded[:, c, k:k + T], scalar=dw[:, c, k:k + 1],
                                                 in1=acc[:, c], op0=ALU.mult, op1=ALU.add)
                if k < TAPS - 1:
                    last[c] = st.mark(ins)
                else:
                    ins.then_inc(acc_ready, 1)

            lanes = [[(c, k) for c in (0, 2) for k in range(TAPS)], [(c, k) for c in (1, 3) for k in range(TAPS)]]
            order = lanes[0][:HEAD_START]
            for one, two in zip(lanes[0][HEAD_START:], lanes[1]):
                order += [one, two]
            order += lanes[1][len(lanes[0]) - HEAD_START:]

            def taps(first, count):
                for c, k in order[first:first + count]:
                    tap(c, k)
                return first + count

            def qk_out(c):
                dve.wait_ge(qk_mm, c + 1)
                v.tensor_tensor(qkT[:, c], b4[:].rearrange("p (w t) -> p w t", w=2),
                                rstd_row.unsqueeze(1).to_broadcast([P, 2, T]), ALU.mult).then_inc(qk_ready, 1)

            def softmax_in(h):
                p, q = h % 2, 2 * (h % 2)
                dve.wait_ge(score_mm, h + 1)
                if h >= 2:
                    dve.wait_ge(probsT_mm, h - 1)
                v.scalar_tensor_tensor(out=probs[:, p, 0:T], in0=hb[p][:, 0:T], scalar=HD ** -0.5,
                                       in1=relb[:, h], op0=ALU.mult, op1=ALU.add)
                v.scalar_tensor_tensor(out=probs[:, p, T:3 * P], in0=hb[p][:, T:3 * P], scalar=HD ** -0.5,
                                       in1=relb[:, h, P:T], op0=ALU.mult, op1=ALU.add).then_inc(score_read, 1)
                dve.wait_ge(score_read, h + 1)
                v.tensor_reduce(negmax[:, q:q + 1], probs[:, p, 0:T], AX.X, ALU.max, negate=True)
                v.tensor_reduce(negmax[:, q + 1:q + 2], probs[:, p, T:3 * P], AX.X, ALU.max,
                                negate=True).then_inc(max_ready, 1)

            def softmax_sum(h):
                q = 2 * (h % 2)
                dve.wait_ge(exp_ready, h + 1)
                v.reciprocal(rden[:, q:q + 2], den[:, q:q + 2]).then_inc(rden_ready, 1)

            conv_in(0)
            n = 0
            conv_gate(0)
            dve.wait_ge(col_mm, 1)
            v.tensor_copy(rstd_col, b6[:, 0:2]).then_inc(col_ready, 1)
            for c, some in ((1, 9), (2, 13), (3, 13)):
                n = taps(n, some)
                conv_in(c)
                n = taps(n, 1)
                conv_gate(c)
            n = taps(n, 36)
            dve.wait_ge(relb_ready, 1)
            for c in range(HEADS // 2):
                qk_out(c)
                n = taps(n, 4)
                for h in (2 * c, 2 * c + 1):
                    softmax_in(h)
                n = taps(n, 5)
                for h in (2 * c, 2 * c + 1):
                    softmax_sum(h)
                n = taps(n, 6)
            dve.wait_ge(acc_ready, CC)
            dve.wait_ge(mu_mm, 1)
            for c in range(CC):
                v.scalar_tensor_tensor(out=acc[:, c], in0=b4[:, 0:T], scalar=-1.0 / D_CONV, in1=acc[:, c],
                                       op0=ALU.mult, op1=ALU.add).then_inc(cent_ready, 1)
            dve.wait_ge(lnv_mm, 1)
            v.tensor_scalar(lnrow[:, 0], b4[:, T:2 * T], 1.0 / D_CONV, EPS, ALU.mult, ALU.add).then_inc(lnv_ready, 1)
            dve.wait_ge(lnsd_ready, 1)
            st.mark(v.reciprocal(lnrow[:, 0], lnrow[:, 0]))
            st.wait()
            for c in range(CC):
                v.tensor_tensor(acc[:, c], acc[:, c], lnrow[:, 0], ALU.mult).then_inc(xn_ready, 1)
            for c in range(CC):
                dve.wait_ge(lnsig_ready, c + 1)
                last[c] = st.mark(v.tensor_scalar(acc[:, c], acc[:, c], ln_g[:, c:c + 1], ln_b[:, c:c + 1],
                                                  ALU.mult, ALU.add))
                if c >= 1:
                    st.wait(last[c - 1])
                    v.tensor_tensor(mixT[:, CC + c - 1], acc[:, c - 1], padded[:, c - 1, 0:T],
                                    ALU.mult).then_inc(conv_ready, 1)
            st.wait()
            v.tensor_tensor(mixT[:, 2 * CC - 1], acc[:, CC - 1], padded[:, CC - 1, 0:T],
                            ALU.mult).then_inc(conv_ready, 1)

            hit4 = hit.rearrange("p (t k) e -> p t k e", t=TT)
            whit4 = whit.rearrange("p (t k) e -> p t k e", t=TT)
            dve.wait_ge(d_gffn, 16)
            dve.wait_ge(d_small, 32)

            def times_gain(t):
                for h in range(2):
                    dve.wait_ge(out_mm, 2 * t + h + 1)
                    v.tensor_tensor(h2[:, t, h * HB:(h + 1) * HB], y[:, 2 * t + h], gain_ffn[:, h * HB:(h + 1) * HB],
                                    ALU.mult).then_inc(gained, 1)

            def second_rms(t):
                dve.wait_ge(ssq_ready, 2 * t + 1)
                v.tensor_scalar(rstd[:, t:t + 1], ssq[:, 2 * t:2 * t + 1], 1.0 / D, EPS, ALU.mult,
                                ALU.add).then_inc(ms_ready, 1)

            def second_rms_inverse(t):
                dve.wait_ge(rms_sd, t + 1)
                v.reciprocal(rstd[:, t:t + 1], rstd[:, t:t + 1]).then_inc(rms_ready, 1)

            def h2T_out(t):
                dve.wait_ge(h2T_mm, 2 * t + 2)
                v.tensor_copy(hT[:, 4:8, t * P:(t + 1) * P],
                              b5[:].rearrange("p (k n) -> p k n", k=4)).then_inc(h2T_dve, 1)

            def logits_T(t):
                dve.wait_ge(lg_mm, t + 1)
                v.tensor_copy(lgT[:, t * P:(t + 1) * P], b6[:, t * P:(t + 1) * P]).then_inc(lgT_ready, 1)

            def top(t):
                dve.wait_ge(lgt_mm, t + 1)
                v.tensor_reduce(lg[:, t], b7[:, t * P:(t + 1) * P].rearrange("p (q e) -> p e q", q=4), AX.X,
                                ALU.add).then_inc(lgt_read, 1)
                dve.wait_ge(lgt_read, t + 1)
                dve.wait_ge(rms_ready, t + 1)
                st.mark(v.scalar_tensor_tensor(out=lg[:, t], in0=lg[:, t], scalar=rstd[:, t:t + 1], in1=router_b[:],
                                               op0=ALU.mult, op1=ALU.add))
                st.wait()
                st.mark(v.max(topv[:, t], lg[:, t]))
                st.wait()
                found = st.mark(v.max_index(topi[:, t], topv[:, t], lg[:, t]))
                v.tensor_tensor(topw[:, t], topv[:, t, 0:TOPK], topv[:, t, 0:1].to_broadcast([P, TOPK]),
                                ALU.subtract).then_inc(top_shift, 1)
                return found

            def chosen(t, found):
                st.wait(found)
                st.mark(v.tensor_copy(topf[:, t], topi[:, t, 0:TOPK]))
                st.wait()
                st.mark(v.tensor_tensor(hit4[:, t], iota[:, 0:E].unsqueeze(1).to_broadcast([P, TOPK, E]),
                                        topf[:, t].unsqueeze(2).to_broadcast([P, TOPK, E]), ALU.is_equal))
                st.wait()
                v.tensor_reduce(mask[:, t], hit4[:, t].rearrange("p k e -> p e k"), AX.X,
                                ALU.add).then_inc(mask_ready, 1)

            times_gain(0)
            second_rms(0)
            second_rms_inverse(0)
            h2T_out(0)
            times_gain(1)
            second_rms(1)
            logits_T(0)
            h2T_out(1)
            found = top(0)
            logits_T(1)
            chosen(0, found)
            second_rms_inverse(1)
            chosen(1, top(1))
            dve.wait_ge(mask_ready, TT)
            v.tensor_copy(mask3.rearrange("p t (c e) -> p t c e", c=EXTRA),
                          mask.unsqueeze(2).to_broadcast([P, TT, EXTRA, E])).then_inc(mask_ready, 1)
            dve.wait_ge(rank_mm, 1)
            counted = b6[:, T:T + TT * E].rearrange("p (t e) -> p t e", t=TT)
            st.mark(v.scalar_tensor_tensor(out=rank[:], in0=counted, scalar=1.0, in1=mask, op0=ALU.add, op1=ALU.mult))
            st.wait()

            def build_sel(e, places, width):
                k = width // CAP
                return v.tensor_tensor(
                    sel[:, :, 0:width].rearrange("p t (k c) -> p t k c", k=k),
                    places.unsqueeze(1).unsqueeze(1).to_broadcast([P, TT, k, CAP]),
                    rank[:, :, bass.ds(e, k)].unsqueeze(3).to_broadcast([P, TT, k, CAP]), ALU.is_equal)

            def build_wsel(e, k):
                v.tensor_tensor(wsel[:, :, 0:k * CAP].rearrange("p t (k c) -> p t k c", k=k),
                                sel[:, :, 0:k * CAP].rearrange("p t (k c) -> p t k c", k=k),
                                share[:, :, bass.ds(e, k)].unsqueeze(3).to_broadcast([P, TT, k, CAP]), ALU.mult)
                return v.tensor_tensor(wsel[:, :, 2 * CAP:3 * CAP], sel[:, :, 0:CAP],
                                       share[:, :, bass.ds(e, 1)].to_broadcast([P, TT, CAP]), ALU.mult)

            def build_pick(e, j):
                src = ident_w[:, bass.ds(e, 4, E)]
                return v.tensor_copy(pick[:, j], src.unsqueeze(2).to_broadcast([P, 4, CAP]))

            build_sel(0, iota[:, 1:CAP + 1], 2 * CAP).then_inc(sel_ready, 1)
            dve.wait_ge(cnt_mm, 1)
            v.tensor_scalar(flag[0:N_LIST], b7[0:N_LIST, 0:1], thresh[0:N_LIST], None,
                            ALU.is_gt).then_inc(flag_ready, 1)
            dve.wait_ge(top_exp, 1)
            st.mark(v.tensor_reduce(wsum, topw, AX.X, ALU.add))
            st.wait()
            st.mark(v.reciprocal(wsum, wsum))
            st.wait()
            st.mark(v.tensor_tensor(topw, topw, wsum.unsqueeze(2).to_broadcast([P, TT, TOPK]), ALU.mult))
            st.wait()
            st.mark(v.tensor_tensor(whit4, hit4, topw.unsqueeze(3).to_broadcast([P, TT, TOPK, E]), ALU.mult))
            st.wait()
            st.mark(v.tensor_reduce(share[:, :, 0:E], whit4.rearrange("p t k e -> p t e k"), AX.X, ALU.add))
            dve.wait_ge(place_mm, 1)
            v.tensor_scalar(onehot[0:N_LIST], iota[0:N_LIST, 0:N_LIST], b7[0:N_LIST, 1:2], flag[0:N_LIST],
                            ALU.is_equal, ALU.mult).then_inc(onehot_ready, 1)
            dve.wait_ge(gath_mm, 1)
            v.tensor_copy(xtok[:, 0:HB], b4[:]).then_inc(xtok_dve, 1)
            st.mark(v.memset(wsel, 0.0))
            st.wait()
            v.tensor_copy(wsel[:, :, 0:E], share[:, :, 0:E])
            v.tensor_copy(wsel[:, :, 2 * CAP:2 * CAP + E], share[:, :, 0:E]).then_inc(wsel_ready, 1)
            for j in range(2):
                ins = build_pick(j, j)
            ins.then_inc(pick_ready, 1)
            for k, o in enumerate((b5, b6)):
                dve.wait_ge(xtokT_mm, k + 1)
                v.tensor_copy(xg[:, 4 * k:4 * k + 4].rearrange("p a b -> p (a b)"), o[:]).then_inc(xg_ready, 1)
            dve.wait_ge(list_mm, 1)
            v.tensor_copy(meta[0:1, 0:2 * N_LIST + 1], b7[0:1, 8:8 + 2 * N_LIST + 1]).then_inc(meta_ready, 1)

            def hidden(n, meanwhile=None):
                dve.wait_ge(gate_mm, (n + 1) * PIECES)
                v.tensor_scalar(gate, b4[:], LIMIT, None, ALU.min).then_inc(gate_ready, 1)
                if meanwhile:
                    meanwhile()
                dve.wait_ge(sig_ready, n + 1)
                v.tensor_tensor(sig, gate, sig, ALU.mult).then_inc(part_ready, 1)
                dve.wait_ge(up_mm, (n + 1) * PIECES)
                v.tensor_scalar(up, b5[:], LIMIT, -LIMIT, ALU.min, ALU.max).then_inc(up_ready, 1)
                dve.wait_ge(part_ready, n + 1)
                dve.wait_ge(up_ready, n + 1)
                v.scalar_tensor_tensor(out=hid, in0=up, scalar=1.0, in1=sig, op0=ALU.add,
                                       op1=ALU.mult).then_inc(hid_ready, 1)

            def weights_of(i):
                dve.wait_ge(wselT_mm, i + 1)
                dve.wait_ge(sel_ready, i + 1)
                build_wsel(i * 2, 2).then_inc(wsel_ready, 1)

            with dve.Fori(0, PAIRS - 1) as i:
                weights_of(i)

                def next_sel():
                    dve.wait_ge(wsel_ready, i + 2)
                    build_sel(i * 2 + 2, iota[:, 1:CAP + 1], 2 * CAP).then_inc(sel_ready, 1)

                hidden(i * 2, next_sel)
                hidden(i * 2 + 1)
                for k in range(2):
                    dve.wait_ge(gath_mm, i * 2 + 3 + k)
                    v.tensor_copy(xg[:, 4 * k:4 * k + 4].rearrange("p a b -> p (a b)"), b4[:]).then_inc(xg_ready, 1)
                for j in range(2):
                    ins = build_pick(i * 2 + 2 + j, j)
                ins.then_inc(pick_ready, 1)
            weights_of(PAIRS - 1)
            for j in range(2):
                hidden(E - 2 + j)
            dve.wait_ge(down_mm, E * PIECES)
            v.tensor_copy(yg[:, 1], b7[:]).then_inc(yg_last, 1)

            def again(m):
                e = expert_of(dve, m)
                first = place_of(dve, m)
                dve.wait_ge(o_scat, m + 1)
                dve.wait_ge(pick_ready, PAIRS)
                build_sel(e, iota[:, bass.ds(first + 1, CAP)], CAP).then_inc(dve_over, 1)
                build_pick(e, 0)
                dve.wait_ge(dve_over, m + 1)
                build_wsel(e, 1).then_inc(o_sel, 1)
                dve.wait_ge(o_gath, m + 1)
                v.tensor_copy(xg[:, :, 0:CAP], b4[:].rearrange("p (k c) -> p k c", k=KT)).then_inc(o_xg, 1)
                dve.wait_ge(o_gate, m + 1)
                v.tensor_scalar(gate, b4[:], LIMIT, None, ALU.min).then_inc(o_gread, 1)
                dve.wait_ge(o_up, m + 1)
                v.tensor_scalar(up, b5[:], LIMIT, -LIMIT, ALU.min, ALU.max)
                dve.wait_ge(o_sig, m + 1)
                v.tensor_tensor(sig, gate, sig, ALU.mult).then_inc(dve_tail, 1)
                dve.wait_ge(dve_tail, m + 1)
                v.scalar_tensor_tensor(out=hid, in0=up, scalar=1.0, in1=sig, op0=ALU.add,
                                       op1=ALU.mult).then_inc(o_hid, 1)

            more_passes(dve, again)
            dve.wait_ge(d_gfin, 16)

            def last_rms(t):
                dve.wait_ge(fsq_ready, 2 * t + 1)
                v.tensor_scalar(frstd[:, t:t + 1], fsq[:, 2 * t:2 * t + 1], 1.0 / D, EPS, ALU.mult,
                                ALU.add).then_inc(fms_ready, 1)

            def last_rms_inverse(t):
                dve.wait_ge(fsd_ready, t + 1)
                st.mark(v.reciprocal(frstd[:, t:t + 1], frstd[:, t:t + 1]))
                st.wait()

            def last_out(t, h):
                v.scalar_tensor_tensor(out=outb[:, t, h * HB:(h + 1) * HB], in0=y[:, 2 * t + h],
                                       scalar=frstd[:, t:t + 1], in1=late[:, h * HB:(h + 1) * HB],
                                       op0=ALU.mult, op1=ALU.mult).then_inc(fin_ready, 1)

            last_rms(0)
            last_rms_inverse(0)
            last_out(0, 0)
            last_rms(1)
            last_out(0, 1)
            last_rms_inverse(1)
            last_out(1, 0)
            last_out(1, 1)

        @block.tensor
        def _(pe):
            def mm(o, l, r, start, stop=False, **kw):
                return pe.matmul(o, l, r, start=start, stop=stop, skip_group_check=True, **kw)

            def seed(h):
                for k in range(4 * h, 4 * h + 4):
                    for t in range(TT):
                        last = pe.matmul(y[:, 2 * t + h, (k % 4) * P:(k % 4 + 1) * P], xT[:, k, t * P:(t + 1) * P],
                                         ident, start=k % 4 == 0, stop=k % 4 == 3, is_transpose=True,
                                         skip_group_check=True)
                return last

            def conv_proj(c, ks):
                for w in range(2):
                    for k in ks:
                        if c == 0 and w == 0:
                            pe.wait_ge(hT_ready, k + 1)
                        last = mm(bank[c][:, w * T:(w + 1) * T], w_conv[:, c, k, w * P:(w + 1) * P], hT[:, k],
                                  w == 0 and k == 0, w == 1 and k == KT - 1)
                return last

            def keep_warm(o, count):
                for _ in range(count):
                    mm(o[:, 0:P], ident, ident, True, True)

            pe.wait_ge(ident_ready, 1)
            keep_warm(b7, WARM_UP)
            for h in range(2):
                pe.wait_ge(d_xT[h], 16)
                last = seed(h)
                if h == 1:
                    last.then_inc(seed_mm, 1)
                pe.wait_ge(d_conv[CC * h], 16)
                last = conv_proj(0, range(4 * h, 4 * h + 4))
            last.then_inc(conv_mm, 1)
            pe.wait_ge(sumsq_ready, 1)
            mm(b7[:, 0:T], ones[:], sumsq, True, True).then_inc(ssum_done, 1)
            for c in range(1, CC):
                if c == 2:
                    pe.wait_ge(norm_ready, 1)
                    for t in range(TT):
                        last = mm(b6[:, t:t + 1], rstd_row[0:1, t * P:(t + 1) * P], ones[0:1, 0:1], True, True)
                    last.then_inc(col_mm, 1)
                    pe.wait_ge(col_ready, 1)
                if c == 3:
                    pe.wait_ge(var_ready, 1)
                pe.wait_ge(d_conv[c], 16)
                conv_proj(c, range(KT)).then_inc(conv_mm, 1)
            pe.wait_ge(d_v, 16)
            for t in range(TT):
                pe.wait_ge(conv_read, t + 1)
                for k in range(KT):
                    last = mm(bank[t][:], hT[:, k, t * P:(t + 1) * P], w_v[:, k], k == 0, k == KT - 1)
                last.then_inc(v_mm, 1)

            def qk_proj(c):
                for w in range(2):
                    for k in range(KT):
                        last = mm(b4[:, w * T:(w + 1) * T], w_qk[:, c, k, w * P:(w + 1) * P], hT[:, k],
                                  k == 0, k == KT - 1)
                last.then_inc(qk_mm, 1)

            def scores(h):
                c, lo, b = h // 2, (h % 2) * HD, hb[h % 2]
                r = slice(lo, lo + HD)
                mm(b[:, 0:T], qkT[r, c, 0, P:T], qkT[r, c, 1, 0:T], True, True)
                mm(b[:, T:3 * P], qkT[r, c, 0, 0:P], qkT[r, c, 1, 0:P], True, True).then_inc(score_mm, 1)

            def probs_T(h):
                pe.wait_ge(probs_ready, h + 1)
                for o, i in ((0, T), (P, 0), (T, P)):
                    last = pe.transpose(hb[h % 2][:, o:o + P], probs[:, h % 2, i:i + P], ident)
                last.then_inc(probsT_mm, 1)

            def weigh_values(c):
                at = (c % 2) * T
                for k in range(TT):
                    for p in range(2):
                        r, hd = slice(p * HD, p * HD + HD), (2 * c + p) * HD
                        last = mm(b7[r, at + k * P:at + T], val[:, k, hd:hd + HD],
                                  probsT[:, p, k * T:T + k * P], k == 0, k == 1)
                last.then_inc(av_mm, 1)

            def out_part(k, t, h):
                return mm(y[:, 2 * t + h], mixT[:, k, t * P:(t + 1) * P], w_out[:, k, h * HB:(h + 1) * HB], False,
                          k == 2 * CC - 1)

            def out_all(k):
                for t in range(TT):
                    for h in range(2):
                        out_part(k, t, h)

            pairs_of_heads = HEADS // 2
            pe.wait_ge(d_qk, 16)
            pe.wait_ge(v_ready, 1)
            for c in range(pairs_of_heads):
                qk_proj(c)
                if c >= 1:
                    for h in (2 * c - 2, 2 * c - 1):
                        probs_T(h)
                if c >= 2:
                    if c == 2:
                        pe.wait_ge(d_wout, 16)
                        pe.wait_ge(av_ready, 1)
                    out_part(0, 0, c % 2)
                pe.wait_ge(qk_ready, c + 1)
                for h in (2 * c, 2 * c + 1):
                    if c == 0:
                        pe.wait_ge(*((v_ready, TT), (conv_read, 3))[h])
                    else:
                        pe.wait_ge(probsT_ready, h - 1)
                    scores(h)
                if c >= 1:
                    pe.wait_ge(probsT_ready, 2 * c)
                    if c == 1:
                        pe.wait_ge(conv_read, 4)
                    if c >= 2:
                        pe.wait_ge(av_ready, c - 1)
                    weigh_values(c - 1)
            for h in range(2):
                out_part(0, 1, h)
            pe.wait_ge(acc_ready, CC)
            for i in range(CC):
                last = mm(b4[:, 0:T], ones[:], acc[:, i], i == 0, i == CC - 1)
            last.then_inc(mu_mm, 1)
            for h in (HEADS - 2, HEADS - 1):
                probs_T(h)
            pe.wait_ge(av_ready, 2)
            out_all(1)
            pe.wait_ge(cent_ready, CC)
            for i in range(CC):
                pe.wait_ge(lnsq_ready, i + 1)
                last = mm(b4[:, T:2 * T], ones[:], lnsq[:, i], i == 0, i == CC - 1)
            last.then_inc(lnv_mm, 1)
            pe.wait_ge(probsT_ready, HEADS)
            pe.wait_ge(av_ready, 3)
            weigh_values(pairs_of_heads - 1)
            out_all(2)
            pe.wait_ge(av_ready, 4)
            out_all(3)

            def h2_T(t):
                for k in range(KT):
                    if k % 4 == 0:
                        pe.wait_ge(gained, 2 * t + k // 4 + 1)
                    last = pe.transpose(bank[k // 4][:, (k % 4) * P:(k % 4 + 1) * P],
                                        h2[:, t, k * P:(k + 1) * P], ident)
                    if k % 4 == 3:
                        last.then_inc(h2T_mm, 1)

            def router(t):
                pe.wait_ge(d_small, 32)
                for r in range(2):
                    pe.wait_ge((h2T_act, h2T_dve)[r], t + 1)
                    for q in range(4):
                        k = 4 * r + q
                        last = mm(b6[32 * q:32 * q + 32, t * P:(t + 1) * P], router_w[:, k],
                                  hT[:, k, t * P:(t + 1) * P], r == 0, r == 1)
                last.then_inc(lg_mm, 1)

            def router_T(t):
                pe.wait_ge(lgT_ready, t + 1)
                if t >= 1:
                    pe.wait_ge(lgt_read, t)
                pe.transpose(b7[:, t * P:(t + 1) * P], lgT[:, t * P:(t + 1) * P], ident).then_inc(lgt_mm, 1)

            for t in range(TT):
                for h in range(2):
                    for k in range(4, 8):
                        if t == 0 and h == 0:
                            pe.wait_ge(conv_ready, k - 3)
                        last = out_part(k, t, h)
                        if (t, h, k) == (1, 1, 4):
                            h2_T(0)
                    last.then_inc(out_mm, 1)
            router(0)
            h2_T(1)
            router_T(0)
            router(1)
            keep_warm(b5, 4)
            router_T(1)
            pe.wait_ge(mask_ready, 1)
            mm(b6[:, T:T + E], before[:], mask[:, 0], True, True)
            mm(b6[:, T + E:T + 2 * E], ones[:], mask[:, 0], True)
            keep_warm(b5, 6)
            pe.wait_ge(mask_ready, 2)
            mm(b6[:, T + E:T + 2 * E], before[:], mask[:, 1], False, True).then_inc(rank_mm, 1)
            pe.wait_ge(mask_ready, 3)
            for t in range(TT):
                last = mm(b7[0:N_LIST, 0:1], mask3[:, t], ones[:, 0:1], t == 0, t == TT - 1)
            last.then_inc(cnt_mm, 1)

            def gather(k, o, width):
                n = HB // width
                for kk in range(n):
                    for t in range(TT):
                        f = (k + kk) * P
                        last = mm(o[:, kk * width:(kk + 1) * width], h2[:, t, f:f + P], sel[:, t, 0:width],
                                  t == 0, t == TT - 1)
                return last

            def weigh_T(o):
                for order in range(2):
                    for t in range(TT):
                        at = (order * TT + t) * P
                        last = pe.transpose(o[:, at:at + P], wsel[:, t, order * CAP:order * CAP + P], ident)
                return last

            def k_tiles(w, waits, count, product, pieces=PIECES, ks=range(KT)):
                for k in ks:
                    for wait in waits.get(k, ()):
                        pe.wait_ge(*wait)
                    last = product(k, w[:, k])
                    if (k + 1) % (KT // pieces) == 0:
                        last.then_inc(count, 1)

            def project(o, lhs, w, waits, bias, j, count, pieces=PIECES):
                def product(k, wk):
                    for h in range(2):
                        last = mm(o[h * CAP:(h + 1) * CAP, :], lhs(k), wk[:, h * HB:(h + 1) * HB], k == 0, k == KT - 1)
                    return last

                k_tiles(w, waits, count, product, pieces, range(PK))
                for h in range(2):
                    mm(o[h * CAP:(h + 1) * CAP, :], pick[:, j, bias + h], bias_gu[:], False)
                k_tiles(w, waits, count, product, pieces, range(PK, KT))

            def down(outs, w, waits, j, count, pieces=PIECES, ks=range(KT)):
                def product(k, wk):
                    for h in range(2):
                        last = down_half(outs, wk, j, k, h)
                    return last

                k_tiles(w, waits, count, product, pieces, ks)

            def down_half(outs, wk, j, k, h):
                q = h ^ j
                return mm(outs[h][q * CAP:(q + 1) * CAP, :], hidT[:, k % 4, (k // 4) * CAP:(k // 4 + 1) * CAP],
                          wk[:, h * HB:(h + 1) * HB], k == 0, k == KT - 1)

            def hid_T(o):
                for c in range(4):
                    last = pe.transpose(o[:, c * P:(c + 1) * P], hid[:, c * P:(c + 1) * P], ident)
                return last

            def scatter(h, ts, weights=wselT, rows=slice(0, P), outputs=yg):
                for t in ts:
                    last = mm(y[:, 2 * t + h], weights[rows, h, t * P:(t + 1) * P], outputs[rows, h], False)
                return last

            pe.wait_ge(h2_ready, TT)
            pe.wait_ge(sel_ready, 1)
            for h in range(2):
                for t in range(TT):
                    last = mm(bank[2 * h][:], sel[:, t], h2[:, t, h * HB:(h + 1) * HB], t == 0, t == TT - 1)
                last.then_inc(gath_mm, 1)
                if h == 0:
                    pe.wait_ge(flag_ready, 1)
                    mm(b7[0:N_LIST, 1:2], before[0:N_LIST, 0:N_LIST], flag[0:N_LIST], True, True).then_inc(place_mm, 1)
            for h, o in enumerate((b5, b6)):
                pe.wait_ge((xtok_dve, xtok_act)[h], 1)
                for k in range(4):
                    last = pe.transpose(o[:, k * P:(k + 1) * P], xtok[:, (4 * h + k) * P:(4 * h + k + 1) * P], ident)
                last.then_inc(xtokT_mm, 1)
            pe.wait_ge(onehot_ready, 1)
            mm(b7[0:1, 8:8 + N_LIST], code_e[0:N_LIST], onehot[0:N_LIST], True, True)
            mm(b7[0:1, 8 + N_LIST:8 + 2 * N_LIST], code_c[0:N_LIST], onehot[0:N_LIST], True, True)
            mm(b7[0:1, 8 + 2 * N_LIST:9 + 2 * N_LIST], flag[0:N_LIST], ones[0:N_LIST, 0:1], True,
               True).then_inc(list_mm, 1)
            pe.wait_ge(wsel_ready, 1)
            pe.wait_ge(xg_ready, 1)
            weigh_T(b5).then_inc(wselT_mm, 1)
            pe.wait_ge(d_bias, 16)

            def loaded(sl, count):
                return {q * PK: [(d_slot[sl][q], count * 16)] for q in range(PIECES)}

            def gate_up(i, j, between=()):
                def tokens(k):
                    return xg[:, k, j * CAP:(j + 1) * CAP]

                waits = loaded(GATE[j], i + 1)
                if j == 0:
                    pe.wait_ge(pick_ready, i + 1)
                    waits[0].append((xg_ready, i * 2 + 1))
                    waits[KT // 2].append((xg_ready, i * 2 + 2))
                project(b4, tokens, slot[:, GATE[j]], waits, 0, j, gate_mm)
                for wait in between:
                    pe.wait_ge(*wait)
                project(b5, tokens, slot[:, UP[j]], loaded(UP[j], i + 1), 2, j, up_mm)

            with pe.Fori(0, PAIRS - 1) as i:
                gate_up(i, 0, [(wselT_ready, i + 1)])
                pe.wait_ge(d_yg, 32)
                scatter(0, range(TT))
                pe.wait_ge(hid_ready, i * 2 + 1)
                hid_T(b5).then_inc(hidT_mm, 1)
                scatter(1, range(TT))
                pe.wait_ge(hidT_ready, i * 2 + 1)
                pe.wait_ge(meta_ready, 1)
                down((b6, b7), slot[:, DOWN], loaded(DOWN, i * 2 + 1), 0, down_mm)
                gate_up(i, 1)
                pe.wait_ge(sel_ready, i + 2)
                pe.wait_ge(gate_ready, i * 2 + 2)
                gather(0, b4, 2 * CAP).then_inc(gath_mm, 1)
                pe.wait_ge(hid_ready, i * 2 + 2)
                hid_T(b5).then_inc(hidT_mm, 1)
                pe.wait_ge(xg_ready, i * 2 + 3)
                gather(4, b4, 2 * CAP).then_inc(gath_mm, 1)
                pe.wait_ge(hidT_ready, i * 2 + 2)
                down((b6, b7), slot[:, DOWN], loaded(DOWN, i * 2 + 2), 1, down_mm)
                pe.wait_ge(wsel_ready, i + 2)
                weigh_T(b5).then_inc(wselT_mm, 1)

            gate_up(PAIRS - 1, 0, [(wselT_ready, PAIRS)])
            scatter(0, range(TT))
            pe.wait_ge(hid_ready, E - 1)
            hid_T(b5).then_inc(hidT_mm, 1)
            scatter(1, range(TT)).then_inc(o_scat, 1)
            pe.wait_ge(wsel_ready, PAIRS + 1)
            weigh_T(b6).then_inc(wselT_mm, 1)
            gate_up(PAIRS - 1, 1, [(hidT_ready, E - 1)])
            pe.wait_ge(wselT_ready, PAIRS + 1)
            down((b6, b7), slot[:, DOWN], loaded(DOWN, E - 1), 0, down_mm)
            pe.wait_ge(hid_ready, E)
            hid_T(b5).then_inc(hidT_mm, 1)
            pe.wait_ge(hidT_ready, E)
            last_w, last_loaded = slot[:, GATE[0]], loaded(GATE[0], PAIRS + 1)
            down((b6, b7), last_w, last_loaded, 1, down_mm, ks=range(KT - PK))
            for k in range(PK):
                at = KT - PK + k
                pe.wait_ge(d_last[k], 16)
                for h in range(2):
                    last = down_half((b6, b7), last_w[:, at], 1, at, h)
                    if k == PK - 1:
                        last.then_inc((half_mm, down_mm)[h], 1)

            def again(m):
                pe.wait_ge(yg_ready, PAIRS)
                pe.wait_ge(yg_last, 1)
                pe.wait_ge(o_sel, m + 1)
                gather(0, b4, CAP).then_inc(o_gath, 1)
                weigh_T(b7).then_inc(o_wselT_mm, 1)
                pe.wait_ge(o_xg, m + 1)
                lhs = lambda k: xg[:, k, 0:CAP]
                whole = lambda k: {0: [(o_slot[k], (m + 1) * 16)]}
                project(b4, lhs, slot[:, 0], whole(0), 0, 0, o_gate, 1)
                project(b5, lhs, slot[:, 1], whole(1), 2, 0, o_up, 1)
                pe.wait_ge(o_hid, m + 1)
                hid_T(b5).then_inc(o_hidT_mm, 1)
                pe.wait_ge(o_hidT, m + 1)
                pe.wait_ge(o_wselT, m + 1)
                down((b6, b7), slot[:, 2], whole(2), 0, o_down, 1)
                pe.wait_ge(o_yg, m + 1)
                scatter(0, range(TT), wselT_more, slice(0, CAP), yg_more)
                scatter(1, range(TT), wselT_more, slice(CAP, P), yg_more).then_inc(o_scat, 1)

            more_passes(pe, again)
            pe.wait_ge(wselT_ready, PAIRS + 1)
            for t in range(TT):
                for h in range(2):
                    pe.wait_ge(*((yg_ready, PAIRS), (yg_last, 1))[h])
                    scatter(h, [t]).then_inc(fin_mm, 1)


_SHAPES = ["xT", "cols", "w_conv", "w_qk", "w_v", "relb", "w_out", "gain_ffn", "router_w", "router_b", "bias_gu",
           "w_gate", "w_up", "w_down", "b_down", "gain_last"]


def _lay_out(x, norm_mix_g, w_in, conv_dw_w, conv_dw_b, conv_ln_g, conv_ln_b, rel_bias, w_out, norm_ffn_g, router_w,
             router_b, exp_w_gate, exp_b_gate, exp_w_up, exp_b_up, exp_w_down, exp_b_down, norm_final_g):
    import numpy as np

    def columns(v):
        return v.reshape(-1, P).T

    def rows(v):
        return np.ascontiguousarray(np.broadcast_to(v, (P, v.shape[-1])))

    w = w_in[0].reshape(KT, P, -1).transpose(1, 0, 2)
    q, k, v, conv, gate = (w[:, :, i * HB:(i + 1) * HB] for i in range(5))

    def pairs(l, r):
        return np.ascontiguousarray(np.stack(
            [np.concatenate([l[:, :, c * P:(c + 1) * P], r[:, :, c * P:(c + 1) * P]], axis=2) for c in range(4)]))

    back = rel_bias[0][:, ::-1]
    ext = np.concatenate([np.repeat(back[:, :1], P - 1, axis=1), back, np.repeat(back[:, -1:], 64, axis=1)], axis=1)
    relb = np.stack([ext[:, P - 1 - p:P - 1 - p + T] for p in range(P)])
    taps = conv_dw_w[0].T.reshape(CC, P, TAPS).transpose(1, 0, 2).reshape(P, CC * TAPS)
    bg, bu = exp_b_gate[0], exp_b_up[0]
    return {
        "xT": x[0].T,
        "cols": np.concatenate([columns(norm_mix_g[0]), taps, columns(conv_dw_b[0]), columns(conv_ln_g[0]),
                                columns(conv_ln_b[0])], axis=1),
        "w_conv": pairs(conv, gate), "w_qk": pairs(q, k), "w_v": v, "relb": relb, "w_out": w_out[0],
        "gain_ffn": rows(norm_ffn_g[0]), "router_w": router_w[0], "router_b": rows(router_b[0]),
        "bias_gu": np.concatenate([bg[:, :HB], bg[:, HB:], bu[:, :HB], bu[:, HB:]], axis=0),
        "w_gate": exp_w_gate[0], "w_up": exp_w_up[0], "w_down": exp_w_down[0], "b_down": exp_b_down[0],
        "gain_last": rows(norm_final_g),
    }


def kernel(**inputs):
    import numpy as np
    import concourse.bacc as bacc
    from concourse.bass_utils import run_bass_kernel_spmd

    laid = _lay_out(**{k: np.asarray(v) for k, v in inputs.items()})
    nc = bacc.Bacc("TRN2", target_bir_lowering=False, num_devices=1)
    arrays, args = {}, {}
    for name in _SHAPES:
        v = np.ascontiguousarray(laid[name])
        arrays[f"in_{name}"] = v
        args[name] = nc.dram_tensor(f"in_{name}", v.shape, mybir.dt.from_np(v.dtype), kind="ExternalInput").ap()
    out = nc.dram_tensor("out_y", (T, D), F32, kind="ExternalOutput").ap()
    build_block(nc, args, out)
    r = run_bass_kernel_spmd(nc, [arrays], core_ids=[0])
    return r.results[0]["out_y"].reshape(1, T, D)
```
